# Optimizing a Trainium2 kernel written in Bass

```python
import math
import jax, jax.numpy as jnp
from jax import lax
import numpy as np

D_MODEL = 1024
BATCH = 1
SEQ = 256
DEPTH = 1

A_HEADS = 8
A_HEAD_DIM = 64
IDX_HEADS = 8
IDX_DIM = 32
TOPK_MAX = 256
Q_BLOCK = 128
REL_BUCKETS = 32
REL_MAX_DIST = 128
B_HEADS = 4
B_KEY_DIM = 128
B_VAL_DIM = 128
CHUNK = 64
N_EXPERTS = 32
TOP_K = 4
D_FF = 1024
SWIGLU_LIMIT = 7.0
SWIGLU_ALPHA = 1.702
EXPERT_BLOCK = 256
EPS = 1e-6

A_WIDTH = A_HEADS * A_HEAD_DIM
B_WIDTH = B_HEADS * B_VAL_DIM
IN_SPLITS = (A_WIDTH, A_WIDTH, A_WIDTH,
             IDX_HEADS * IDX_DIM, IDX_HEADS, IDX_DIM,
             B_HEADS * B_KEY_DIM, B_HEADS * B_KEY_DIM,
             B_WIDTH, B_WIDTH,
             D_MODEL, D_MODEL)
IN_WIDTH = sum(IN_SPLITS)

kernel_name = "hybrid_dsa_hgrn2_moe_block"

def rmsnorm(x, gain):
    xf = x.astype(jnp.float32)
    y = xf * lax.rsqrt(jnp.mean(xf * xf, axis=-1, keepdims=True) + EPS)
    return (y * gain.astype(jnp.float32)).astype(x.dtype)

def t5_bucket(dist):
    n = jnp.maximum(dist, 0)
    max_exact = REL_BUCKETS // 2
    nf = jnp.maximum(n, 1).astype(jnp.float32)
    large = max_exact + (jnp.log(nf / max_exact) / math.log(REL_MAX_DIST / max_exact)
                         * (REL_BUCKETS - max_exact)).astype(jnp.int32)
    large = jnp.minimum(large, REL_BUCKETS - 1)
    return jnp.where(n < max_exact, n, large)

def dsa_sparse_attention(q, k, v, q_idx, w_idx, k_idx, rel_bias):
    B, S, H, Dh = q.shape
    topk = min(TOPK_MAX, S // 4)
    n_blocks = S // Q_BLOCK
    scale = A_HEAD_DIM ** -0.5
    idx_scale = IDX_DIM ** -0.5
    w_scaled = w_idx.astype(jnp.float32) * (IDX_HEADS ** -0.5)
    key_pos = jnp.arange(S, dtype=jnp.int32)
    bidx = jnp.arange(B)[:, None, None]

    def block(i):
        start = i * Q_BLOCK
        qb = lax.dynamic_slice_in_dim(q, start, Q_BLOCK, axis=1)
        qib = lax.dynamic_slice_in_dim(q_idx, start, Q_BLOCK, axis=1)
        wb = lax.dynamic_slice_in_dim(w_scaled, start, Q_BLOCK, axis=1)
        qpos = start + jnp.arange(Q_BLOCK, dtype=jnp.int32)
        s_h = jnp.einsum('bqhd,bsd->bqhs', qib, k_idx,
                         preferred_element_type=jnp.float32) * idx_scale
        score = jnp.einsum('bqhs,bqh->bqs', jax.nn.relu(s_h), wb)
        causal = key_pos[None, :] <= qpos[:, None]
        score = jnp.where(causal[None], score, -jnp.inf)
        _, sel = lax.top_k(score, topk)
        kg = k[bidx, sel]
        vg = v[bidx, sel]
        logits = jnp.einsum('bqhd,bqkhd->bqhk', qb, kg,
                            preferred_element_type=jnp.float32) * scale
        dist = qpos[None, :, None] - sel
        bias = rel_bias[t5_bucket(dist)].astype(jnp.float32)
        logits = logits + jnp.transpose(bias, (0, 1, 3, 2))
        logits = jnp.where((dist >= 0)[:, :, None, :], logits, -jnp.inf)
        p = jax.nn.softmax(logits, axis=-1).astype(v.dtype)
        return jnp.einsum('bqhk,bqkhd->bqhd', p, vg)

    out = lax.map(block, jnp.arange(n_blocks))
    return jnp.transpose(out, (1, 0, 2, 3, 4)).reshape(B, S, H * Dh)

def hgrn2_chunkwise(q_raw, f_raw, i_in, lb):
    B, S, H, Dk = q_raw.shape
    Dv = i_in.shape[-1]
    n_chunks = S // CHUNK
    f = lb + (1.0 - lb) * jax.nn.sigmoid(f_raw.astype(jnp.float32))
    g = jnp.log(f)
    kk = 1.0 - f
    qq = jax.nn.silu(q_raw.astype(jnp.float32)) * (Dk ** -0.5)
    vv = i_in.astype(jnp.float32)

    def to_chunks(t):
        return t.reshape(B, n_chunks, CHUNK, H, t.shape[-1]).transpose(1, 0, 3, 2, 4)

    mask = jnp.tril(jnp.ones((CHUNK, CHUNK), dtype=bool))

    def step(state, xs):
        qc, kc, vc, gc = xs
        b = jnp.cumsum(gc, axis=2)
        o_inter = jnp.einsum('bhcd,bhde->bhce', qc * jnp.exp(b), state)
        rel = jnp.where(mask[None, None, :, :, None],
                        b[:, :, :, None, :] - b[:, :, None, :, :], -jnp.inf)
        attn = jnp.einsum('bhtd,bhsd,bhtsd->bhts', qc, kc, jnp.exp(rel))
        o_intra = jnp.einsum('bhts,bhse->bhte', attn, vc)
        b_last = b[:, :, -1:, :]
        new_state = (jnp.exp(b_last[:, :, 0, :])[..., None] * state
                     + jnp.einsum('bhsd,bhse->bhde', kc * jnp.exp(b_last - b), vc))
        return new_state, o_inter + o_intra

    s0 = jnp.zeros((B, H, Dk, Dv), jnp.float32)
    _, o = lax.scan(step, s0, (to_chunks(qq), to_chunks(kk), to_chunks(vv), to_chunks(g)))
    return o.transpose(1, 0, 3, 2, 4).reshape(B, S, H, Dv)

def moe_ffn(h, w_router, b_router, w_gu, b_gu, w_down, b_down):
    B, S, D = h.shape
    T = B * S
    xt = h.reshape(T, D)
    logits = (xt @ w_router).astype(jnp.float32) + b_router.astype(jnp.float32)
    top_val, top_idx = lax.top_k(logits, TOP_K)
    gates = jax.nn.softmax(top_val, axis=-1)
    A = T * TOP_K
    e_flat = top_idx.reshape(A)
    order = jnp.argsort(e_flat)
    e_sorted = e_flat[order]
    tok_sorted = (order // TOP_K).astype(jnp.int32)
    counts = jnp.bincount(e_flat, length=N_EXPERTS)
    starts = jnp.cumsum(counts) - counts
    padded = (counts + EXPERT_BLOCK - 1) // EXPERT_BLOCK * EXPERT_BLOCK
    pad_ends = jnp.cumsum(padded)
    pad_starts = pad_ends - padded
    dest = pad_starts[e_sorted] + (jnp.arange(A) - starts[e_sorted])
    n_blocks = -(-A // EXPERT_BLOCK) + N_EXPERTS
    P = n_blocks * EXPERT_BLOCK
    buf_tok = jnp.full((P,), T, dtype=jnp.int32).at[dest].set(tok_sorted)
    block_expert = jnp.minimum(
        jnp.searchsorted(pad_ends, jnp.arange(n_blocks) * EXPERT_BLOCK, side='right'),
        N_EXPERTS - 1)
    x_pad = jnp.concatenate([xt, jnp.zeros((1, D), xt.dtype)], axis=0)

    def expert_block(args):
        toks, e = args
        xb = x_pad[toks]
        gu = xb @ w_gu[e] + b_gu[e]
        gate, lin = gu[:, :D_FF], gu[:, D_FF:]
        gate = jnp.minimum(gate, SWIGLU_LIMIT)
        lin = jnp.clip(lin, -SWIGLU_LIMIT, SWIGLU_LIMIT)
        act = (lin + 1.0) * gate * jax.nn.sigmoid(SWIGLU_ALPHA * gate)
        return act @ w_down[e] + b_down[e]

    y_buf = lax.map(expert_block, (buf_tok.reshape(n_blocks, EXPERT_BLOCK), block_expert))
    y_buf = y_buf.reshape(P, D)
    y_assign = jnp.zeros((A, D), y_buf.dtype).at[order].set(y_buf[dest])
    y = jnp.einsum('tkd,tk->td', y_assign.reshape(T, TOP_K, D), gates.astype(y_buf.dtype))
    return y.reshape(B, S, D)

def setup_inputs(seed: int = 0) -> dict:
    key = jax.random.key(seed)
    ks = jax.random.split(key, 18)
    nrm = jax.random.normal
    f32 = jnp.float32
    return {
        "x": nrm(ks[0], (BATCH, SEQ, D_MODEL), f32),
        "w_in": nrm(ks[1], (DEPTH, D_MODEL, IN_WIDTH), f32) * D_MODEL ** -0.5,
        "w_up_a": nrm(ks[2], (DEPTH, A_WIDTH, D_MODEL), f32) * A_WIDTH ** -0.5,
        "w_up_b": nrm(ks[3], (DEPTH, B_WIDTH, D_MODEL), f32) * B_WIDTH ** -0.5,
        "w_out": nrm(ks[4], (DEPTH, D_MODEL, D_MODEL), f32) * D_MODEL ** -0.5,
        "norm_mix": 1.0 + 0.1 * nrm(ks[5], (DEPTH, D_MODEL), f32),
        "norm_ffn": 1.0 + 0.1 * nrm(ks[6], (DEPTH, D_MODEL), f32),
        "norm_final": 1.0 + 0.1 * nrm(ks[7], (D_MODEL,), f32),
        "hgrn_norm": 1.0 + 0.1 * nrm(ks[8], (DEPTH, B_HEADS, B_VAL_DIM), f32),
        "lb_logits": 0.5 * nrm(ks[9], (DEPTH + 1, B_HEADS * B_KEY_DIM), f32),
        "rel_bias": 0.5 * nrm(ks[10], (REL_BUCKETS, A_HEADS), f32),
        "w_router": nrm(ks[11], (DEPTH, D_MODEL, N_EXPERTS), f32) * D_MODEL ** -0.5,
        "b_router": 0.01 * nrm(ks[12], (DEPTH, N_EXPERTS), f32),
        "w_gu": nrm(ks[13], (DEPTH, N_EXPERTS, D_MODEL, 2 * D_FF), f32) * D_MODEL ** -0.5,
        "b_gu": 0.01 * nrm(ks[14], (DEPTH, N_EXPERTS, 2 * D_FF), f32),
        "w_down": nrm(ks[15], (DEPTH, N_EXPERTS, D_FF, D_MODEL), f32) * D_FF ** -0.5,
        "b_down": 0.01 * nrm(ks[16], (DEPTH, N_EXPERTS, D_MODEL), f32),
    }

def reference(x, w_in, w_up_a, w_up_b, w_out, norm_mix, norm_ffn, norm_final, hgrn_norm,
              lb_logits, rel_bias, w_router, b_router, w_gu, b_gu, w_down, b_down):
    B, S, _ = x.shape
    split_points = [int(p) for p in np.cumsum(IN_SPLITS)[:-1]]
    lb_all = jnp.cumsum(jax.nn.softmax(lb_logits.astype(jnp.float32), axis=0), axis=0)
    for l in range(DEPTH):
        h = rmsnorm(x, norm_mix[l])
        proj = h @ w_in[l]
        (aq, ak, av, iq, iw, ik, bq, bf, bi, bg, ga, gb) = jnp.split(proj, split_points, axis=-1)
        y_a = dsa_sparse_attention(
            aq.reshape(B, S, A_HEADS, A_HEAD_DIM),
            ak.reshape(B, S, A_HEADS, A_HEAD_DIM),
            av.reshape(B, S, A_HEADS, A_HEAD_DIM),
            iq.reshape(B, S, IDX_HEADS, IDX_DIM), iw, ik, rel_bias)
        lb = lb_all[l].reshape(B_HEADS, B_KEY_DIM)
        o_b = hgrn2_chunkwise(bq.reshape(B, S, B_HEADS, B_KEY_DIM),
                              bf.reshape(B, S, B_HEADS, B_KEY_DIM),
                              bi.reshape(B, S, B_HEADS, B_VAL_DIM), lb)
        o_b = rmsnorm(o_b, hgrn_norm[l]) * jax.nn.silu(
            bg.reshape(B, S, B_HEADS, B_VAL_DIM).astype(jnp.float32))
        y_b = o_b.reshape(B, S, B_WIDTH).astype(x.dtype)
        merged = (jax.nn.sigmoid(ga) * (y_a @ w_up_a[l])
                  + jax.nn.sigmoid(gb) * (y_b @ w_up_b[l]))
        x = x + merged @ w_out[l]
        x = x + moe_ffn(rmsnorm(x, norm_ffn[l]), w_router[l], b_router[l],
                        w_gu[l], b_gu[l], w_down[l], b_down[l])
    return rmsnorm(x, norm_final)


_drawn_inputs = setup_inputs


def setup_inputs(seed=0):
    import zlib

    import numpy as np

    out = dict(_drawn_inputs(seed))
    spreads = {}
    factors = {'b_gu': 8.0, 'b_down': 8.0}
    for name, (base, spread) in spreads.items():
        noise = np.random.default_rng([zlib.crc32(name.encode()), seed]).standard_normal(out[name].shape)
        drawn = base * np.exp(spread * noise) if base else spread * noise
        out[name] = __import__('jax').numpy.asarray(drawn.astype(out[name].dtype))
    for name, factor in factors.items():
        out[name] = (out[name] * factor).astype(out[name].dtype)
    return out
```

```python
import math
from contextlib import ExitStack

import numpy as np
import concourse.bass as bass
from concourse import mybir

F32 = mybir.dt.float32
I32 = mybir.dt.int32
U32 = mybir.dt.uint32
ALU = mybir.AluOpType
ACT = mybir.ActivationFunctionType
AX = mybir.AxisListType

P = 128
D, S = 1024, 256
NT = S // P
NJ = D // P
AH, AD = 8, 64
IH, ID = 8, 32
TOPK = min(256, S // 4)
BH, BD = 4, 128
NE, TOP_K, FF = 32, 4, 1024
BUCKETS, MAX_DIST = 32, 128
EPS = 1e-6
LIMIT, ALPHA = 7.0, 1.702
SLOTS = 64
MAX_ITEMS = NE + S * TOP_K // SLOTS
TAB = 64
NONCAUSAL = -3.0e38
TAKEN = -3.3e38
DROPPED = -1.0e30
PITCH = S + P - 1

IN_COLS = {"iq": 1536, "aq": 0, "ak": 512, "av": 1024, "bq": 1832, "bf": 2344, "bi": 2856,
           "bg": 3368, "ga0": 3880, "ga1": 4392, "gb0": 4904, "gb1": 5416}
ORDER = ["iq", "aq", "ak", "av", "bq", "bf", "bi", "bg", "ga0", "ga1", "gb0", "gb1"]
IDX_W = IH * ID + IH + ID
RING = 6
CHUNK = 4096
N_PRE = len(ORDER) + 4
PRE_USES = [len(range(s, N_PRE, RING)) for s in range(RING)]
LEVELS = 7


def slot_of(chunk):
    return chunk % RING


MOE_SLOT = [slot_of(N_PRE + c) for c in range(RING)]


def t5_bucket(dist):
    exact = BUCKETS // 2
    if dist < exact:
        return max(dist, 0)
    return min(exact + int(math.log(dist / exact) / math.log(MAX_DIST / exact) * (BUCKETS - exact)),
               BUCKETS - 1)


def shape_constants():
    i = np.arange(P)
    cols = np.zeros((P, 4), np.float32)
    cols[:, 0] = i - NE
    cols[:, 1] = np.where(i < NE, i, 0)
    cols[:, 2] = i >= NE
    cols[:, 3] = -0.5
    consts = np.concatenate([
        np.eye(P), i[:, None] < i[None, :], np.ones((P, P)),
        np.where(i[None, :] <= i[:, None], 0.0, NONCAUSAL),
        np.broadcast_to(np.arange(S), (P, S)), cols], axis=1).astype(np.float32)
    levels = np.zeros((P, LEVELS, P // 2), np.int32)
    for l in range(LEVELS):
        size = 1 << l
        odd = i[(i // size) % 2 == 1]
        levels[:, l, :] = ((i[:, None] // (2 * size) == odd[None, :] // (2 * size))
                           & ((i[:, None] // size) % 2 == 0))
    onehot = np.zeros((BUCKETS, PITCH + 1), np.float32)
    for c in range(PITCH):
        onehot[t5_bucket(S - 1 - c), c] = 1.0
    return consts, levels.reshape(P, LEVELS * P // 2), onehot


def build(nc, x, w_in, w_up_a, w_up_b, w_out, norm_mix, norm_ffn, norm_final, hgrn_norm, lb_logits,
          rel_bias, w_router, b_router, w_gu, b_gu, w_down, b_down, consts, levels, onehot, out):
    ctx = ExitStack()
    with ctx:
        def sb(name, words, dt=F32, parts=P):
            return ctx.enter_context(nc.sbuf_tensor(name, [parts, words], dt))

        def sem(name):
            return ctx.enter_context(nc.semaphore(name))

        ring = ctx.enter_context(nc.sbuf_tensor("ring", [P, RING, CHUNK], F32))
        x_sb = sb("x_sb", NT * D)
        hT_region = sb("hT_region", NJ * S)
        work = sb("work", NT * D)
        work0 = sb("work0", AH * P)
        qk_region = sb("qk_region", 3072)
        va_region = sb("va_region", NT * 512)
        idx_region = sb("idx_region", 1536)
        score = sb("score", S + P)
        hg = sb("hg", 4096)
        vb_region = sb("vb_region", NT * 512)
        silu_g = sb("silu_g", BH * S)
        sig_a = sb("sig_a", NJ * S)
        sig_b = sb("sig_b", NJ * S)
        bias_region = sb("bias_region", 3072)
        wr_sb = sb("wr_sb", NJ * NE)
        cst = sb("cst", 4 * P + S + 4)
        lvl = sb("lvl", LEVELS * P // 2, I32)
        tiny = sb("tiny", 544)
        itiny = sb("itiny", 8 * NT, U32)
        table = score[0:1, 0:2 * TAB + 1].bitcast(I32)
        psum = ctx.enter_context(nc.psum_tensor("psum", [P, 8, 512], F32))
        rel_rows = nc.dram_tensor("rel_rows", (AH, P, PITCH + 1), F32)

        def banks(a, b):
            return psum[:, a:b, :].rearrange("p b n -> p (b n)")

        ident, before, ones, noncausal = (cst[:, i * P:(i + 1) * P] for i in range(4))
        iota = cst[:, 4 * P:4 * P + S]
        over_idx, first_expert, is_over, minus_half = (
            cst[:, 4 * P + S + i:4 * P + S + i + 1] for i in range(4))

        xr = x_sb[:, :].rearrange("p (r d) -> p r d", r=NT)
        hT = hT_region[:, :].rearrange("p (j t) -> p j t", j=NJ)
        mergedT = hT
        perm = work[:, :].rearrange("p (r j q) -> p r j q", r=NT, j=NJ)
        relu1 = work[:, :].rearrange("p (h s) -> p h s", h=AH)
        relu0 = work0[:, :].rearrange("p (h s) -> p h s", h=AH)
        probs = {0: relu0, 1: relu1}
        qT = qk_region[:, 0:1024].rearrange("p (m t) -> p m t", m=4)
        kblk = qk_region[:, 1024:3072].rearrange("p (m a t) -> p m a t", m=4, a=2)
        mixT = qk_region[:, 0:1024].rearrange("p (g t) -> p g t", t=P)
        crossT = qk_region[:, 1024:1536].rearrange("p (h t) -> p h t", h=BH)
        y_aT = qk_region[:, 2048:3072].rearrange("p (m t) -> p m t", m=4)
        v_a = va_region[:, :].rearrange("p (r c) -> p r c", r=NT)
        iqT = idx_region[:, 0:512].rearrange("p (m t) -> p m t", m=2)
        ikblk = idx_region[:, 512:1536].rearrange("p (g t) -> p g t", g=4)
        score1, score0 = score[:, 0:S], score[:, S:S + P]
        hq, hk, hf, hprod = (hg[:, i * 1024:(i + 1) * 1024] for i in range(4))
        v_b = vb_region[:, :].rearrange("p (r c) -> p r c", r=NT)
        bias1 = bias_region[:, 0:2048].rearrange("p (h s) -> p h s", h=AH)
        bias0 = bias_region[:, 2048:3072].rearrange("p (h s) -> p h s", h=AH)
        pT0 = bias_region[:, 0:2048].rearrange("p (h q) -> p h q", h=AH)
        pT1 = bias_region[:, 2048:3072].rearrange("p (h q) -> p h q", h=AH)
        bias_gu, bias_dn = bias_region[:, 0:2048], bias_region[:, 2048:3072]
        oh_dist = hprod[0:BUCKETS, 0:PITCH + 1]
        rel_sb = hprod[0:BUCKETS, 512:512 + AH]
        rel_row = hprod[0:AH, 576:576 + PITCH + 1]
        gate_sb, lin_sb, sig_sb, act_sb, actT_sb, y_sb, combT_sb, xgT_sb = (
            hg[:, i * 512:(i + 1) * 512] for i in range(8))
        pick = idx_region[:, 0:128].rearrange("p (r s) -> p r s", r=NT)
        padded = idx_region[:, 128:512].rearrange("p (r s) -> p r s", r=NT)
        which_expert = idx_region[:, 512:576]
        h2 = perm
        h2T = hT

        at = [0]

        def take(n):
            at[0] += n
            return tiny[:, at[0] - n:at[0]]

        g_mix, ss, rs = take(NJ), take(NT), take(NT)
        lb0, lb1, lbm, lb, lb_rest = (take(BH) for _ in range(5))
        tiny_lb = tiny[:, at[0] - 5 * BH:at[0] - 3 * BH]
        g_hgrn = take(BH)
        w_idx = take(NT * IH).rearrange("p (r h) -> p r h", r=NT)
        top8 = take(8)
        row_max, den = {r: take(AH) for r in range(NT)}, {r: take(AH) for r in range(NT)}
        o_ss, o_rs = take(NT * BH), take(NT * BH)
        router_b = take(NE)
        r_logits = take(NT * NE).rearrange("p (r e) -> p r e", r=NT)
        r_top = take(NT * 8).rearrange("p (r k) -> p r k", r=NT)
        r_idx = take(NT * 8).rearrange("p (r k) -> p r k", r=NT)
        r_neg, r_den = take(NT), take(NT)
        r_gate = take(NT * TOP_K).rearrange("p (r k) -> p r k", r=NT)
        sel = take(NT * NE).rearrange("p (r e) -> p r e", r=NT)
        gates = take(NT * NE).rearrange("p (r e) -> p r e", r=NT)
        pos = take(NT * NE).rearrange("p (r e) -> p r e", r=NT)
        n_over, cum, le, items = take(NE), take(NE), take(NE), take(4)
        choice = work0[:, 0:256].rearrange("p (r k e) -> p r k e", r=NT, k=TOP_K)
        choice_g = work0[:, 256:512].rearrange("p (r k e) -> p r k e", r=NT, k=TOP_K)
        zeros32 = work0[:, 512:544]
        merge_a, merge_b = work0[:, 0:256], work0[:, 256:512]

        x_in, consts_in, params_in, rel_in = sem("x_in"), sem("consts_in"), sem("params_in"), sem("rel_in")
        rel_stored, bias_in = sem("rel_stored"), sem("bias_in")
        w_in_slot = [sem(f"w_loaded{s}") for s in range(RING)]
        w_used = [sem(f"w_used{s}") for s in range(RING)]
        squares, rs_ready, pool_step = sem("squares"), sem("rs_ready"), sem("pool_step")
        xn_ready, xT_done, hT_ready = sem("xn_ready"), sem("xT_done"), sem("hT_ready")
        blocks_zero = sem("blocks_zero")
        evacuated = [sem("evacuated0"), sem("evacuated1")]
        rel_done, rel_row_ready = sem("rel_done"), sem("rel_row_ready")
        sig_ready = sem("sig_ready")
        score_mm, relu_ready, masks_ready, bias_ready = (
            sem("score_mm"), sem("relu_ready"), sem("masks_ready"), sem("bias_ready"))
        logits_mm, logits_ready, max_ready, exp_ready, probs_ready = (
            sem("logits_mm"), sem("logits_ready"), sem("max_ready"), sem("exp_ready"), sem("probs_ready"))
        probsT_mm, probsT_ready, ya_mm, ya_ready = (
            sem("probsT_mm"), sem("probsT_ready"), sem("ya_mm"), sem("ya_ready"))
        lb_shifted, lb_exp, dve_step = sem("lb_shifted"), sem("lb_exp"), sem("dve_step")
        hgrn_ready, diag_mm, level_ready, level_mm, mix_ready = (
            sem("hgrn_ready"), sem("diag_mm"), sem("level_ready"), sem("level_mm"), sem("mix_ready"))
        o_mm, o_copied, o_squares, o_rs_ready, o_normed, yb_mm, yb_ready = (
            sem(n) for n in ("o_mm", "o_copied", "o_squares", "o_rs_ready", "o_normed",
                             "yb_mm", "yb_ready"))
        merge_mm, merge_ready, out_mm, x_new = (
            sem("merge_mm"), sem("merge_ready"), sem("out_mm"), sem("x_new"))
        ffn_gain_in, moe_bias_zero, moe_bias_in, final_gain_in = (
            sem(n) for n in ("ffn_gain_in", "moe_bias_zero", "moe_bias_in", "final_gain_in"))
        h2T_ready = [sem("h2T_ready0"), sem("h2T_ready1")]
        h2_ready, h2T_mm, router_mm, router_max, router_exp, sel_ready, pos_mm = (
            sem(n) for n in ("h2_ready", "h2T_mm", "router_mm", "router_max",
                             "router_exp", "sel_ready", "pos_mm"))
        items_ready, items_mm, table_ready, padded_zero = (
            sem(n) for n in ("items_ready", "items_mm", "table_ready", "padded_zero"))
        pick_ready, padded_ready, gate_ready, act_ready = (
            sem(n) for n in ("pick_ready", "padded_ready", "gate_ready", "act_ready"))
        sigm_ready, xg_ready, actT_ready, combT_ready, y_ready = (
            sem(n) for n in ("sigm_ready", "xg_ready", "actT_ready", "combT_ready", "y_ready"))
        gather_mm, actT_mm, combT_mm, y_mm, all_mm = (
            sem(n) for n in ("gather_mm", "actT_mm", "combT_mm", "y_mm", "all_mm"))
        moe_dve = sem("moe_dve")
        final_ss, final_rs, out_ready, out_stored = (
            sem(n) for n in ("final_ss", "final_rs", "out_ready", "out_stored"))

        w_in_v = w_in[0].rearrange("(p j) n -> p j n", j=NJ)
        up_v = [w[0].rearrange("(m p) n -> p m n", p=P) for w in (w_up_a, w_up_b)]
        out_v = w_out[0].rearrange("(m p) n -> p m n", p=P)
        gu_v = w_gu[0].rearrange("e (p j) n -> e p j n", j=NJ)
        down_v = w_down[0].rearrange("e (m p) n -> e p m n", p=P)

        def slot_in(n):
            w = IDX_W if n == 0 else 512
            return ring[:, slot_of(n), 0:NJ * w].rearrange("p (j n) -> p j n", j=NJ)

        def slot4(s):
            return ring[:, s, :].rearrange("p (m n) -> p m n", m=4)

        def slot_gu(c):
            return ring[:, MOE_SLOT[c], :].rearrange("p (j n) -> p j n", j=2)

        block = ctx.enter_context(nc.Block())

        @block.sync
        def _(sp):
            for r in range(NT):
                sp.dma_start(xr[:, r, :], x[0, r * P:(r + 1) * P, :]).then_inc(x_in, 16)
            for n in range(N_PRE):
                s = slot_of(n)
                if n == 1:
                    sp.wait_ge(consts_in, 32)
                    sp.wait_ge(rel_in, 32)
                    sp.wait_ge(params_in, 80)
                if n >= RING:
                    sp.wait_ge(w_used[s], n // RING)
                if n < len(ORDER):
                    c0 = IN_COLS[ORDER[n]]
                    w = IDX_W if n == 0 else 512
                    sp.dma_start(slot_in(n), w_in_v[:, :, c0:c0 + w]).then_inc(w_in_slot[s], 16)
                elif n < len(ORDER) + 2:
                    sp.dma_start(slot4(s), up_v[n - len(ORDER)]).then_inc(w_in_slot[s], 16)
                else:
                    m0 = 4 * (n - len(ORDER) - 2)
                    sp.dma_start(slot4(s), out_v[:, m0:m0 + 4, :]).then_inc(w_in_slot[s], 16)

            def load_item(e, i, first=False):
                for c in range(RING):
                    s = MOE_SLOT[c]
                    if c == RING - 1:
                        if first:
                            sp.wait_ge(out_mm, NT)
                        else:
                            sp.wait_ge(y_mm, i + 1)
                    else:
                        sp.wait_ge(w_used[s], i + PRE_USES[s])
                    if c < 4:
                        src = gu_v[bass.ds(e, 1), :, 2 * c:2 * c + 2, :].rearrange("e p j n -> (e p) j n")
                        sp.dma_start(slot_gu(c), src).then_inc(w_in_slot[s], 16)
                    else:
                        m0 = 4 * (c - 4)
                        src = down_v[bass.ds(e, 1), :, m0:m0 + 4, :].rearrange("e p m n -> (e p) m n")
                        sp.dma_start(slot4(s), src).then_inc(w_in_slot[s], 16)

            load_item(0, 0, True)
            sp.wait_ge(table_ready, 1)
            n_items = sp.value_load(table[0:1, 2 * TAB:2 * TAB + 1], min_val=NE, max_val=MAX_ITEMS)
            with sp.Fori(1, n_items) as i:
                e = sp.value_load(table[0:1, bass.ds(i, 1)], min_val=0, max_val=NE - 1)
                load_item(e, i)
            for r in range(NT):
                sp.wait_ge(out_ready, r + 1)
                sp.dma_start(out[0, r * P:(r + 1) * P, :], xr[:, r, :]).then_inc(out_stored, 16)
            sp.wait_ge(out_stored, 16 * NT)

        @block.tensor
        def _(pe):
            mm = nc.tensor.matmul

            def transposes(src, bank0, done):
                for r in range(NT):
                    pe.wait_ge(*src(r))
                    dst = banks(bank0 + 2 * r, bank0 + 2 * r + 2).rearrange("p (j t) -> p j t", j=NJ)
                    for j in range(NJ):
                        last = nc.tensor.transpose(dst[:, j, :], perm[:, r, j, :], ident)
                    last.then_inc(done, 1)

            def half_T(n, half):
                w, b = slot_in(n), 2 * (n % 2) + half
                for c in range(2):
                    for j in range(NJ):
                        last = mm(psum[:, b, c * S:(c + 1) * S], w[:, j, (2 * half + c) * P:(2 * half + c + 1) * P],
                                  hT[:, j, :], start=(j == 0), stop=(j == NJ - 1))
                return last

            def half_tok(n, half):
                w, b = slot_in(n), 2 * (n % 2) + half
                for j in range(NJ):
                    last = mm(psum[:, b, :], hT[:, j, half * P:(half + 1) * P], w[:, j, :],
                              start=(j == 0), stop=(j == NJ - 1))
                return last

            def project(n, half):
                if half == 0:
                    pe.wait_ge(w_in_slot[slot_of(n)], 16 * (n // RING + 1))
                    if n >= 2:
                        pe.wait_ge(evacuated[n % 2], n // 2)
                form = half_tok if ORDER[n] in ("av", "bi") else half_T
                last = form(n, half)
                if half:
                    last.then_inc(w_used[slot_of(n)], 1)

            pe.wait_ge(rel_in, 32)
            mm(psum[0:AH, 7, 0:PITCH + 1], rel_sb, oh_dist, start=True, stop=True).then_inc(rel_done, 1)

            pe.wait_ge(consts_in, 32)
            transposes(lambda r: (xn_ready, r + 1), 0, xT_done)
            pe.wait_ge(hT_ready, NT)

            pe.wait_ge(w_in_slot[0], 16)
            w0 = slot_in(0)
            for m in range(2):
                for j in range(NJ):
                    mm(psum[:, 0, m * S:(m + 1) * S], w0[:, j, m * P:(m + 1) * P], hT[:, j, :],
                       start=(j == 0), stop=(j == NJ - 1))
            for j in range(NJ):
                for g in range(4):
                    mm(psum[32 * g:32 * g + 32, 1, 0:S], w0[:, j, IH * ID + IH:IDX_W], hT[:, j, :],
                       start=(j == 0), stop=(j == NJ - 1))
            for r in range(NT):
                for j in range(NJ):
                    last = mm(psum[:, 1, S + r * IH:S + (r + 1) * IH], hT[:, j, r * P:(r + 1) * P],
                              w0[:, j, IH * ID:IH * ID + IH], start=(j == 0), stop=(j == NJ - 1))
            last.then_inc(w_used[0], 1)

            def scores(r):
                keys = (r + 1) * P
                group = 512 // keys
                for m in range(2):
                    for g in range(4 // group):
                        last = mm(psum[:, 4 + m * (4 // group) + g, 0:group * keys], iqT[:, m, r * P:(r + 1) * P],
                                  ikblk[:, g * group:(g + 1) * group, 0:keys], start=True, stop=True)
                last.then_inc(score_mm, 1)

            def logits(r):
                keys = (r + 1) * P
                for m in range(4):
                    dst = banks(4, 8)[:, m * 2 * keys:(m + 1) * 2 * keys]
                    last = mm(dst, qT[:, m, r * P:(r + 1) * P], kblk[:, m, :, 0:keys], start=True, stop=True)
                last.then_inc(logits_mm, 1)

            def probs_T(rnd):
                dst = banks(4, 6).rearrange("p (g q) -> p g q", q=P)
                for g in range(8):
                    src = probs[0][:, g, :] if rnd == 2 else \
                        probs[1][:, 4 * rnd + g // 2, (g % 2) * P:(g % 2 + 1) * P]
                    last = nc.tensor.transpose(dst[:, g, :], src, ident)
                last.then_inc(probsT_mm, 1)

            def values():
                dst = banks(4, 6).rearrange("p (m q) -> p m q", m=4)
                for h in range(AH):
                    rows = slice((h % 2) * AD, (h % 2 + 1) * AD)
                    cols = slice(h * AD, (h + 1) * AD)
                    mm(dst[rows, h // 2, :], v_a[:, 0, cols], pT0[:, h, :], start=True, stop=False)
                    last = mm(dst[rows, h // 2, P:S], v_a[:, 1, cols], pT1[:, h, :], start=False, stop=True)
                last.then_inc(ya_mm, 1)

            def diagonal():
                dst = banks(6, 8).rearrange("p (g t) -> p g t", t=P)
                for g in range(BH * NT):
                    cols = slice(g * P, (g + 1) * P)
                    last = mm(dst[:, g, :], hk[:, cols], hq[:, cols], start=True, stop=True)
                last.then_inc(diag_mm, 1)

            def level(l):
                pe.wait_ge(level_ready, l + 1)
                dst = psum[:, 6 + l % 2, :]
                if l < LEVELS:
                    for g in range(BH * NT):
                        odd = hq[:, g * P:(g + 1) * P].rearrange("p (n a l) -> p a n l", a=2, l=1 << l)[:, 1]
                        last = mm(dst[:, g * 64:(g + 1) * 64], hk[:, g * P:(g + 1) * P], odd, start=True, stop=True)
                else:
                    for h in range(BH):
                        last = mm(dst[:, h * P:(h + 1) * P], hk[:, h * S:h * S + P], hq[:, h * S + P:(h + 1) * S],
                                  start=True, stop=True)
                last.then_inc(level_mm, 1)

            project(1, 0)
            project(1, 1)
            pe.wait_ge(evacuated[0], 1)
            scores(1)
            project(2, 0)
            project(2, 1)
            pe.wait_ge(relu_ready, 1)
            scores(0)
            for n in (3, 4, 5):
                project(n, 0)
                project(n, 1)
            pe.wait_ge(relu_ready, 2)
            pe.wait_ge(evacuated[1], 1)
            pe.wait_ge(evacuated[0], 2)
            logits(1)
            project(6, 0)
            pe.wait_ge(logits_ready, 1)
            logits(0)
            project(6, 1)
            pe.wait_ge(hgrn_ready, 1)
            diagonal()
            project(7, 0)
            level(0)
            project(7, 1)
            level(1)
            pe.wait_ge(probs_ready, 1)
            pe.wait_ge(logits_ready, 2)
            probs_T(0)
            project(8, 0)
            level(2)
            pe.wait_ge(probsT_ready, 1)
            probs_T(1)
            project(8, 1)
            level(3)
            pe.wait_ge(probs_ready, 2)
            pe.wait_ge(probsT_ready, 2)
            probs_T(2)
            project(9, 0)
            level(4)
            pe.wait_ge(probsT_ready, 3)
            pe.wait_ge(evacuated[1], 2)
            values()
            project(9, 1)
            level(5)
            project(10, 0)
            level(6)
            project(10, 1)
            level(7)
            project(11, 0)
            pe.wait_ge(mix_ready, 1)
            pe.wait_ge(evacuated[0], 4)
            for h in range(BH):
                cols = slice(h * P, (h + 1) * P)
                mm(psum[:, 6, cols], mixT[:, h * NT, :], v_b[:, 0, cols], start=True, stop=True)
                mm(psum[:, 7, cols], crossT[:, h, :], v_b[:, 0, cols], start=True, stop=False)
                last = mm(psum[:, 7, cols], mixT[:, h * NT + 1, :], v_b[:, 1, cols], start=False, stop=True)
            last.then_inc(o_mm, 1)
            project(11, 1)
            pe.wait_ge(o_normed, 1)
            ob = hq.rearrange("p (r h e) -> p r h e", r=NT, h=BH)
            dst = banks(6, 8).rearrange("p (h t) -> p h t", h=BH)
            for h in range(BH):
                for r in range(NT):
                    last = nc.tensor.transpose(dst[:, h, r * P:(r + 1) * P], ob[:, r, h, :], ident)
            last.then_inc(yb_mm, 1)

            y_bT = hf.rearrange("p (h t) -> p h t", h=BH)
            for m in range(NJ):
                s = [slot_of(len(ORDER)), slot_of(len(ORDER) + 1)]
                if m == 0:
                    pe.wait_ge(evacuated[0], len(ORDER) // 2)
                    pe.wait_ge(evacuated[1], len(ORDER) // 2)
                    pe.wait_ge(ya_ready, 1)
                    pe.wait_ge(w_in_slot[s[0]], 16 * (len(ORDER) // RING + 1))
                    pe.wait_ge(w_in_slot[s[1]], 16 * (len(ORDER) // RING + 1))
                if m >= 4:
                    pe.wait_ge(merge_ready, m - 3)
                for k in range(4):
                    last = mm(psum[:, m % 4, 0:S], slot4(s[0])[:, k, m * P:(m + 1) * P], y_aT[:, k, :],
                              start=(k == 0), stop=(k == 3))
                if m == NJ - 1:
                    last.then_inc(w_used[s[0]], 1)
                if m == 0:
                    pe.wait_ge(yb_ready, 1)
                for k in range(4):
                    last = mm(psum[:, m % 4, S:2 * S], slot4(s[1])[:, k, m * P:(m + 1) * P], y_bT[:, k, :],
                              start=(k == 0), stop=(k == 3))
                last.then_inc(merge_mm, 1)
            for r in range(NT):
                for m in range(NJ):
                    s = slot_of(len(ORDER) + 2 + m // 4)
                    if r == 0:
                        if m % 4 == 0:
                            pe.wait_ge(w_in_slot[s], 16 * (len(ORDER) // RING + 1))
                        pe.wait_ge(merge_ready, m + 1)
                    for half in range(2):
                        last = mm(psum[:, 4 + 2 * r + half, :], mergedT[:, m, r * P:(r + 1) * P],
                                  slot4(s)[:, m % 4, half * 512:(half + 1) * 512],
                                  start=(m == 0), stop=(m == NJ - 1), skip_group_check=True)
                        if m == 0 and r == 0 and half == 0:
                            last.then_inc(w_used[slot_of(len(ORDER) + 1)], 1)
                    if r == NT - 1 and m == 3:
                        last.then_inc(w_used[s], 1)
                last.then_inc(out_mm, 1)

            for r in range(NT):
                pe.wait_ge(h2_ready, r + 1)
                dst = banks(2 * r, 2 * r + 2).rearrange("p (j t) -> p j t", j=NJ)
                for j in range(NJ):
                    last = nc.tensor.transpose(dst[:, j, :], h2[:, r, j, :], ident)
                last.then_inc(h2T_mm, 1)
            for r in range(NT):
                pe.wait_ge(h2T_ready[r], r + 1)
                for j in range(NJ):
                    last = mm(psum[:, 2 * r, 0:NE], h2T[:, j, r * P:(r + 1) * P],
                              wr_sb[:, j * NE:(j + 1) * NE], start=(j == 0), stop=(j == NJ - 1))
                last.then_inc(router_mm, 1)
            for r in range(NT):
                for half in range(2):
                    last = mm(psum[:, 4 + 2 * r + half, :], ident, xr[:, r, half * 512:(half + 1) * 512],
                              start=True, stop=True, skip_group_check=True)
            last.then_inc(y_mm, 1)
            pe.wait_ge(sel_ready, 1)
            mm(psum[:, 1, 0:NE], before, sel[:, 0, :], start=True, stop=True)
            mm(psum[:, 1, NE:2 * NE], ones, sel[:, 0, :], start=True, stop=False)
            mm(psum[:, 1, NE:2 * NE], before, sel[:, 1, :], start=False, stop=True)
            mm(psum[:, 1, 2 * NE:3 * NE], ones, sel[:, 0, :], start=True, stop=False)
            mm(psum[:, 1, 2 * NE:3 * NE], ones, sel[:, 1, :], start=False, stop=True).then_inc(pos_mm, 1)
            pe.wait_ge(items_ready, 1)
            mm(psum[0:1, 0, 0:P], items[:, 0:1], ident, start=True, stop=True)
            mm(psum[0:1, 0, P:2 * P], items[:, 1:2], ident, start=True, stop=True).then_inc(items_mm, 1)

            def gather(part):
                for j in range(4 * part, 4 * part + 4):
                    for r in range(NT):
                        last = mm(psum[:, 3, j * SLOTS:(j + 1) * SLOTS], h2[:, r, j, :], pick[:, r, :],
                                  start=(r == 0), stop=(r == NT - 1))
                return last

            def combine(r):
                for half in range(2):
                    last = mm(psum[:, 4 + 2 * r + half, :], combT_sb[:, (half * NT + r) * P:(half * NT + r + 1) * P],
                              y_sb, start=False, stop=True, skip_group_check=True)
                return last

            pe.wait_ge(pick_ready, 1)
            gather(0)
            gather(1).then_inc(gather_mm, 1)
            pe.wait_ge(moe_bias_in, 32)
            pe.wait_ge(table_ready, 1)
            n_items = pe.value_load(table[0:1, 2 * TAB:2 * TAB + 1], min_val=NE, max_val=MAX_ITEMS)
            with pe.Fori(0, n_items) as i:
                pe.wait_ge(xg_ready, i + 1)
                for c in range(4):
                    s = MOE_SLOT[c]
                    pe.wait_ge(w_in_slot[s], (i + PRE_USES[s] + 1) * 16)
                    for jj in range(2):
                        j = 2 * c + jj
                        for b in range(2):
                            for half in range(2):
                                c0 = b * FF + half * 512
                                last = mm(psum[half * 64:half * 64 + 64, b, :], xgT_sb[:, j * SLOTS:(j + 1) * SLOTS],
                                          slot_gu(c)[:, jj, c0:c0 + 512], start=(j == 0), stop=(j == NJ - 1),
                                          skip_group_check=True)
                    last.then_inc(w_used[s], 1)
                    if c == 0:
                        pe.wait_ge(padded_ready, i + 1)
                        for b in range(2):
                            for half in range(2):
                                c0 = b * FF + half * 512
                                mm(psum[half * 64:half * 64 + 64, b, :], which_expert, bias_gu[:, c0:c0 + 512],
                                   start=False, stop=False, skip_group_check=True)
                    if c == 2:
                        pe.wait_ge(combT_ready, i + 1)
                        pe.wait_ge(pick_ready, i + 2)
                        gather(0)
                pe.wait_ge(y_ready, i + 1)
                combine(0)
                combine(1)
                pe.wait_ge(act_ready, i + 1)
                for c in range(4):
                    last = nc.tensor.transpose(psum[:, 2, c * P:(c + 1) * P], act_sb[:, c * P:(c + 1) * P], ident)
                last.then_inc(actT_mm, 1)
                gather(1).then_inc(gather_mm, 1)
                pe.wait_ge(actT_ready, i + 1)
                for half in range(2):
                    mm(psum[half * 64:half * 64 + 64, 2, :], which_expert, bias_dn[:, half * 512:(half + 1) * 512],
                       start=True, stop=False, skip_group_check=True)
                for c in range(4, RING):
                    s = MOE_SLOT[c]
                    pe.wait_ge(w_in_slot[s], (i + PRE_USES[s] + 1) * 16)
                    for k in range(4):
                        m = 4 * (c - 4) + k
                        a = (m % 4) * P + (m // 4) * SLOTS
                        for half in range(2):
                            last = mm(psum[half * 64:half * 64 + 64, 2, :], actT_sb[:, a:a + SLOTS],
                                      slot4(s)[:, k, half * 512:(half + 1) * 512], start=False, stop=(m == NJ - 1),
                                      skip_group_check=True)
                    if c == 4:
                        last.then_inc(w_used[s], 1)
                        pe.wait_ge(xg_ready, i + 2)
                        for q in range(2 * NT):
                            a = (1 - q // NT) * SLOTS
                            tr = nc.tensor.transpose(psum[:, 3, q * P:(q + 1) * P], padded[:, q % NT, a:a + P], ident)
                        tr.then_inc(combT_mm, 1)
                last.then_inc(y_mm, 1)
            pe.wait_ge(y_ready, n_items + 1)
            pe.wait_ge(combT_ready, n_items + 1)
            for r in range(NT):
                combine(r).then_inc(all_mm, 1)

        @block.scalar
        def _(act):
            f = nc.scalar.activation
            for dst, src, s in [
                (cst[:, :], consts, consts_in), (lvl[:, :], levels, consts_in),
                (oh_dist, onehot, rel_in), (rel_sb, rel_bias, rel_in),
                (g_mix, norm_mix[0].rearrange("(p j) -> p j", j=NJ), params_in),
                (tiny_lb, lb_logits, params_in), (g_hgrn, hgrn_norm, params_in),
                (router_b, b_router.partition_broadcast(P).rearrange("p a e -> p (a e)"), params_in),
                (wr_sb[:, :], w_router[0].rearrange("(p j) e -> p (j e)", j=NJ), params_in),
            ]:
                act.dma_start(dst, src).then_inc(s, 16)
            junk = hT_region[:, 0:D]
            for r in range(NT):
                act.wait_ge(x_in, 32)
                f(junk, xr[:, r, :], ACT.Square, accum_out=ss[:, r:r + 1]).then_inc(squares, 1)
                act.wait_ge(squares, r + 1)
            act.wait_ge(rel_row_ready, 1)
            act.dma_start(rel_rows.ap(), rel_row.unsqueeze(1).broadcast_to([AH, P, PITCH + 1])).then_inc(rel_stored, 16)
            act.wait_ge(lb_shifted, 1)
            f(tiny_lb, tiny_lb, ACT.Exp).then_inc(lb_exp, 1)
            act.wait_ge(rel_stored, 16)
            for r, dst in ((1, bias1), (0, bias0)):
                keys = (r + 1) * P
                src = bass.AP(rel_rows, S - 1 - r * P, [[PITCH, P], [P * (PITCH + 1), AH], [1, keys]])
                act.dma_start(dst, src).then_inc(bias_in, 16)

            def chunk_done(n):
                act.wait_ge(w_used[slot_of(n)], n // RING + 1)

            def proj(n):
                return banks(2 * (n % 2), 2 * (n % 2) + 2)

            chunk_done(1)
            f(qk_region[:, 0:1024], proj(1), ACT.Copy).then_inc(evacuated[1], 1)
            act.wait_ge(score_mm, 1)
            f(work[:, :], banks(4, 8), ACT.Relu, scale=ID ** -0.5).then_inc(relu_ready, 1)
            act.wait_ge(score_mm, 2)
            f(work0[:, :], banks(4, 6), ACT.Relu, scale=ID ** -0.5).then_inc(relu_ready, 1)
            chunk_done(3)
            f(va_region[:, :], proj(3), ACT.Copy).then_inc(evacuated[1], 1)
            chunk_done(4)
            f(hq, proj(4), ACT.Sigmoid).then_inc(sig_ready, 1)
            chunk_done(5)
            f(hf, proj(5), ACT.Sigmoid).then_inc(evacuated[1], 1)
            for n, r in enumerate((1, 0)):
                act.wait_ge(max_ready, n + 1)
                for h in range(AH):
                    last = f(probs[r][:, h, :], probs[r][:, h, :], ACT.Exp, bias=row_max[r][:, h:h + 1],
                             accum_out=den[r][:, h:h + 1])
                last.then_inc(exp_ready, 1)
            chunk_done(6)
            f(vb_region[:, :], proj(6), ACT.Copy).then_inc(evacuated[0], 1)
            chunk_done(7)
            f(silu_g[:, :], proj(7), ACT.Sigmoid).then_inc(sig_ready, 1)
            for rnd in range(2):
                act.wait_ge(probsT_mm, rnd + 1)
                src = banks(4, 6).rearrange("p (h s q) -> p h s q", h=4, s=2)
                f(pT0[:, 4 * rnd:4 * rnd + 4, P:S], src[:, :, 0, :], ACT.Copy)
                f(pT1[:, 4 * rnd:4 * rnd + 4, :], src[:, :, 1, :], ACT.Copy).then_inc(probsT_ready, 1)
            chunk_done(8)
            f(sig_a[:, 0:1024], proj(8), ACT.Sigmoid).then_inc(evacuated[0], 1)
            act.wait_ge(probsT_mm, 3)
            f(pT0[:, :, 0:P], banks(4, 6).rearrange("p (h q) -> p h q", h=AH), ACT.Copy).then_inc(probsT_ready, 1)
            act.wait_ge(ya_mm, 1)
            f(qk_region[:, 2048:3072], banks(4, 6), ACT.Copy).then_inc(ya_ready, 1)
            act.dma_start(va_region[:, :], norm_ffn[0].partition_broadcast(P)).then_inc(ffn_gain_in, 16)
            chunk_done(9)
            f(sig_a[:, 1024:2048], proj(9), ACT.Sigmoid).then_inc(evacuated[1], 1)
            act.wait_ge(moe_bias_zero, 1)
            act.dma_start(bias_gu[0:NE, :], b_gu[0]).then_inc(moe_bias_in, 16)
            act.dma_start(bias_dn[0:NE, :], b_down[0]).then_inc(moe_bias_in, 16)
            chunk_done(10)
            f(sig_b[:, 0:1024], proj(10), ACT.Sigmoid).then_inc(evacuated[0], 1)
            act.wait_ge(o_mm, 1)
            f(hq, banks(6, 8), ACT.Copy).then_inc(o_copied, 1)
            act.dma_start(vb_region[:, :], norm_final.partition_broadcast(P)).then_inc(final_gain_in, 16)
            chunk_done(11)
            f(sig_b[:, 1024:2048], proj(11), ACT.Sigmoid).then_inc(evacuated[1], 1)
            for r in range(NT):
                act.wait_ge(x_new, r + 1)
                f(sig_a[:, 0:D], xr[:, r, :], ACT.Square, accum_out=ss[:, r:r + 1]).then_inc(squares, 1)
                act.wait_ge(squares, NT + r + 1)
            act.wait_ge(h2T_mm, 2)
            f(h2T[:, 0:4, P:S], psum[:, 2, :].rearrange("p (j t) -> p j t", j=4), ACT.Copy).then_inc(h2T_ready[1], 1)
            act.wait_ge(router_max, 1)
            for r in range(NT):
                last = f(r_gate[:, r, :], r_top[:, r, 0:TOP_K], ACT.Exp, bias=r_neg[:, r:r + 1],
                         accum_out=r_den[:, r:r + 1])
            last.then_inc(router_exp, 1)
            act.wait_ge(gather_mm, 1)
            f(xgT_sb, psum[:, 3, :], ACT.Copy).then_inc(xg_ready, 1)
            act.wait_ge(table_ready, 1)
            n_items = act.value_load(table[0:1, 2 * TAB:2 * TAB + 1], min_val=NE, max_val=MAX_ITEMS)
            with act.Fori(0, n_items) as i:
                act.wait_ge(gate_ready, i + 1)
                f(sig_sb, gate_sb, ACT.Sigmoid, scale=ALPHA).then_inc(sigm_ready, 1)
                act.wait_ge(actT_mm, i + 1)
                f(actT_sb, psum[:, 2, :], ACT.Copy).then_inc(actT_ready, 1)
                act.wait_ge(gather_mm, i + 2)
                f(xgT_sb, psum[:, 3, :], ACT.Copy).then_inc(xg_ready, 1)
                act.wait_ge(combT_mm, i + 1)
                f(combT_sb, psum[:, 3, :], ACT.Copy).then_inc(combT_ready, 1)
                act.wait_ge(y_mm, i + 2)
                f(y_sb, psum[:, 2, :], ACT.Copy).then_inc(y_ready, 1)
            for r in range(NT):
                act.wait_ge(all_mm, r + 1)
                f(hT_region[:, r * D:(r + 1) * D], banks(4 + 2 * r, 6 + 2 * r), ACT.Square,
                  accum_out=ss[:, r:r + 1]).then_inc(final_ss, 1)

        @block.vector
        def _(dve):
            v = nc.vector
            steps = [0]

            def link(ins):
                steps[0] += 1
                ins.then_inc(dve_step, 1)
                dve.wait_ge(dve_step, steps[0])

            def bc(ap, shape):
                return ap.broadcast_to(shape)

            dve.wait_ge(rel_done, 1)
            v.tensor_copy(rel_row, psum[0:AH, 7, 0:PITCH + 1]).then_inc(rel_row_ready, 1)
            dve.wait_ge(params_in, 80)
            link(v.tensor_tensor(lbm, lb0, lb1, ALU.max))
            v.tensor_tensor(lb0, lb0, lbm, ALU.subtract)
            v.tensor_tensor(lb1, lb1, lbm, ALU.subtract).then_inc(lb_shifted, 1)
            dve.wait_ge(x_in, 32)
            for r in range(NT):
                dve.wait_ge(rs_ready, r + 1)
                v.tensor_scalar(perm[:, r], xr[:, r, :].rearrange("p (q j) -> p j q", j=NJ), rs[:, r:r + 1], None,
                                ALU.mult).then_inc(xn_ready, 1)
            for r in range(NT):
                dve.wait_ge(xT_done, r + 1)
                v.tensor_tensor(hT[:, :, r * P:(r + 1) * P], banks(2 * r, 2 * r + 2).rearrange("p (j t) -> p j t", j=NJ),
                                bc(g_mix.unsqueeze(2), [P, NJ, P]), ALU.mult).then_inc(hT_ready, 1)
            dve.wait_ge(lb_exp, 1)
            link(v.tensor_tensor(lbm, lb0, lb1, ALU.add))
            link(v.reciprocal(lbm, lbm))
            link(v.tensor_tensor(lb, lb0, lbm, ALU.mult))
            v.tensor_scalar(lb_rest, lb, -1.0, 1.0, ALU.mult, ALU.add)

            def chunk_done(n):
                dve.wait_ge(w_used[slot_of(n)], n // RING + 1)

            def proj(n):
                return banks(2 * (n % 2), 2 * (n % 2) + 2)

            chunk_done(0)
            dve.wait_ge(blocks_zero, 2)
            v.tensor_copy(idx_region[:, 0:512], psum[:, 0, :])
            for g in range(4):
                rows = slice(32 * g, 32 * g + 32)
                v.tensor_copy(ikblk[rows, g, :], psum[rows, 1, 0:S])
            v.tensor_scalar(w_idx, psum[:, 1, S:S + NT * IH].rearrange("p (r h) -> p r h", r=NT), IH ** -0.5, None,
                            ALU.mult).then_inc(evacuated[0], 1)
            dve.wait_ge(evacuated[0], 1)

            def top_keys(n, r, sc, relu):
                dve.wait_ge(relu_ready, n)
                link(v.tensor_scalar(sc, relu[:, 0, :], w_idx[:, r, 0:1], None, ALU.mult))
                for h in range(1, IH):
                    link(v.scalar_tensor_tensor(sc, relu[:, h, :], w_idx[:, r, h:h + 1], sc, ALU.mult, ALU.add))
                own = sc[:, r * P:(r + 1) * P]
                link(v.tensor_tensor(own, own, noncausal, ALU.add))
                for _ in range(TOPK // 8):
                    link(v.max(top8, sc))
                    link(v.match_replace(sc, top8, sc, TAKEN))
                link(v.tensor_scalar(sc, sc, TAKEN, DROPPED, ALU.not_equal, ALU.mult))
                v.tensor_tensor(own, own, noncausal, ALU.add).then_inc(masks_ready, 1)

            top_keys(1, 1, score1, relu1)
            chunk_done(2)
            for a in range(2):
                rows = slice(a * AD, (a + 1) * AD)
                last = v.tensor_copy(kblk[rows, :, a, :], proj(2)[rows, :].rearrange("p (m t) -> p m t", m=4))
            last.then_inc(evacuated[0], 1)
            top_keys(2, 0, score0, relu0)

            dve.wait_ge(sig_ready, 1)
            v.scalar_tensor_tensor(hq, proj(4), BD ** -0.5, hq, ALU.mult, ALU.mult).then_inc(evacuated[0], 1)
            dve.wait_ge(evacuated[1], 3)
            for h in range(BH):
                fh = hf[:, h * S:(h + 1) * S]
                last = v.tensor_scalar(fh, fh, lb_rest[:, h:h + 1], lb[:, h:h + 1], ALU.mult, ALU.add)
            link(last)
            v.tensor_scalar(hk, hf, -1.0, 1.0, ALU.mult, ALU.add).then_inc(hgrn_ready, 1)

            for n, (r, bias) in enumerate(((1, bias1), (0, bias0))):
                keys = (r + 1) * P
                dve.wait_ge(logits_mm, n + 1)
                dve.wait_ge(bias_ready, n + 1)
                v.scalar_tensor_tensor(probs[r], banks(4, 8)[:, 0:AH * keys].rearrange("p (h s) -> p h s", h=AH),
                                       AD ** -0.5, bias, ALU.mult, ALU.add).then_inc(logits_ready, 1)
                dve.wait_ge(logits_ready, n + 1)
                link(v.tensor_reduce(row_max[r], probs[r], AX.X, ALU.max))
                v.tensor_scalar(row_max[r], row_max[r], -1.0, None, ALU.mult).then_inc(max_ready, 1)

            dve.wait_ge(diag_mm, 1)
            dve.wait_ge(consts_in, 32)
            link(v.tensor_tensor(mixT, banks(6, 8).rearrange("p (g t) -> p g t", t=P),
                                 bc(ident.unsqueeze(1), [P, BH * NT, P]), ALU.mult))
            v.tensor_tensor(hq, hq, hf, ALU.mult).then_inc(level_ready, 1)
            dve.wait_ge(level_ready, 1)
            offset = [0]
            products = hf

            def next_level(l, products):
                dve.wait_ge(level_mm, l + 1)
                size = 1 << l
                if l == LEVELS:
                    v.tensor_copy(crossT, psum[:, 6 + l % 2, :].rearrange("p (h t) -> p h t", h=BH)).then_inc(mix_ready, 1)
                    return None
                odd = mixT.rearrange("p g (n a l) -> p g n a l", a=2, l=size)[:, :, :, 1, :]
                mask = lvl[:, l * 64:(l + 1) * 64].rearrange("p (n l) -> p n l", l=size)
                data = psum[:, 6 + l % 2, :].rearrange("p (g n l) -> p g n l", g=BH * NT, l=size)
                n = 64 // size
                v.copy_predicated(odd, bc(mask.unsqueeze(1), [P, BH * NT, n, size]), data)
                pairs = products.rearrange("p (n a) -> p n a", a=2)
                nb = 512 // size
                q2 = hq.rearrange("p (n a l) -> p n a l", a=2, l=size)
                k2 = hk.rearrange("p (n a l) -> p n a l", a=2, l=size)
                grown = hprod[:, offset[0]:offset[0] + nb]
                offset[0] += nb
                v.tensor_tensor(q2[:, :, 1, :], q2[:, :, 1, :], bc(pairs[:, :, 0:1], [P, nb, size]), ALU.mult)
                v.tensor_tensor(grown, pairs[:, :, 0], pairs[:, :, 1], ALU.mult)
                v.tensor_tensor(k2[:, :, 0, :], k2[:, :, 0, :], bc(pairs[:, :, 1:2], [P, nb, size]),
                                ALU.mult).then_inc(level_ready, 1)
                dve.wait_ge(level_ready, l + 2)
                return grown

            def normalise(n, r):
                keys = (r + 1) * P
                dve.wait_ge(exp_ready, n)
                link(v.reciprocal(den[r], den[r]))
                v.tensor_tensor(probs[r], probs[r], bc(den[r].unsqueeze(2), [P, AH, keys]),
                                ALU.mult).then_inc(probs_ready, 1)

            products = next_level(0, products)
            normalise(1, 1)
            products = next_level(1, products)
            dve.wait_ge(sig_ready, 2)
            v.tensor_tensor(silu_g[:, :], proj(7), silu_g[:, :], ALU.mult).then_inc(evacuated[1], 1)
            normalise(2, 0)
            for l in range(2, LEVELS + 1):
                products = next_level(l, products)

            dve.wait_ge(o_copied, 1)
            link(v.tensor_tensor(hk, hq, hq, ALU.mult))
            v.tensor_reduce(o_ss, hk.rearrange("p (g e) -> p g e", e=BD), AX.X, ALU.add).then_inc(o_squares, 1)
            dve.wait_ge(o_rs_ready, 1)
            o3 = hq.rearrange("p (g e) -> p g e", e=BD)
            v.tensor_tensor(o3, o3, bc(o_rs.unsqueeze(2), [P, NT * BH, BD]), ALU.mult).then_inc(o_normed, 1)
            dve.wait_ge(yb_mm, 1)
            for h in range(BH):
                cols = slice(h * S, (h + 1) * S)
                last = v.scalar_tensor_tensor(hf[:, cols], banks(6, 8)[:, cols], g_hgrn[:, h:h + 1], silu_g[:, cols],
                                              ALU.mult, ALU.mult)
            last.then_inc(yb_ready, 1)

            for n in range(2):
                dve.wait_ge(evacuated[n], len(ORDER) // 2)
            for m in range(NJ):
                cols = slice(m * S, (m + 1) * S)
                dve.wait_ge(merge_mm, m + 1)
                if m:
                    dve.wait_ge(merge_ready, m)
                v.tensor_tensor(merge_a, psum[:, m % 4, 0:S], sig_a[:, cols], ALU.mult)
                link(v.tensor_tensor(merge_b, psum[:, m % 4, S:2 * S], sig_b[:, cols], ALU.mult))
                v.tensor_tensor(mergedT[:, m, :], merge_a, merge_b, ALU.add).then_inc(merge_ready, 1)
            dve.wait_ge(ffn_gain_in, 16)
            for r in range(NT):
                dve.wait_ge(out_mm, r + 1)
                v.tensor_tensor(xr[:, r, :], xr[:, r, :], banks(4 + 2 * r, 6 + 2 * r), ALU.add).then_inc(x_new, 1)
                dve.wait_ge(x_new, r + 1)
                dve.wait_ge(rs_ready, NT + r + 1)
                v.scalar_tensor_tensor(h2[:, r], xr[:, r, :].rearrange("p (q j) -> p j q", j=NJ), rs[:, r:r + 1],
                                       va_region[:, :].rearrange("p (q j) -> p j q", j=NJ), ALU.mult,
                                       ALU.mult).then_inc(h2_ready, 1)
            dve.wait_ge(h2T_mm, 1)
            v.tensor_copy(h2T[:, :, 0:P], banks(0, 2).rearrange("p (j t) -> p j t", j=NJ)).then_inc(h2T_ready[0], 1)
            dve.wait_ge(h2T_mm, 2)
            v.tensor_copy(h2T[:, 4:8, P:S], psum[:, 3, :].rearrange("p (j t) -> p j t", j=4)).then_inc(h2T_ready[1], 1)

            dve.wait_ge(router_mm, NT)
            link(v.tensor_tensor(r_logits, psum[:, 0:2 * NT:2, 0:NE],
                                 bc(router_b.unsqueeze(1), [P, NT, NE]), ALU.add))
            for r in range(NT):
                link(v.max(r_top[:, r, :], r_logits[:, r, :]))
                link(v.max_index(itiny[:, r * 8:(r + 1) * 8], r_top[:, r, :], r_logits[:, r, :]))
            v.tensor_scalar(r_neg, r_top[:, :, 0], -1.0, None, ALU.mult).then_inc(router_max, 1)
            link(v.tensor_copy(r_idx, itiny[:, 0:NT * 8].rearrange("p (r k) -> p r k", r=NT)))
            for r in range(NT):
                last = v.tensor_tensor(choice[:, r], bc(iota[:, 0:NE].unsqueeze(1), [P, TOP_K, NE]),
                                       bc(r_idx[:, r, 0:TOP_K].unsqueeze(2), [P, TOP_K, NE]), ALU.is_equal)
            link(last)
            for r in range(NT):
                last = v.tensor_reduce(sel[:, r, :], choice[:, r].rearrange("p k e -> p e k"), AX.X, ALU.add)
            last.then_inc(sel_ready, 1)
            dve.wait_ge(sel_ready, 1)
            link(v.tensor_scalar(pos, sel, -1.0e4, 1.0e4, ALU.mult, ALU.add))
            dve.wait_ge(pos_mm, 1)
            link(v.tensor_tensor(pos, pos, psum[:, 1, 0:NT * NE].rearrange("p (r e) -> p r e", r=NT), ALU.add))
            for r in range(NT):
                last = v.tensor_scalar(pick[:, r, :], iota[:, 0:SLOTS], pos[:, r, 0:1], None, ALU.is_equal)
            last.then_inc(pick_ready, 1)
            counts = psum[:, 1, 2 * NE:3 * NE]
            link(v.tensor_scalar(n_over, counts, float(SLOTS), None, ALU.is_gt))
            for c in range(2, S // SLOTS):
                link(v.scalar_tensor_tensor(n_over, counts, float(c * SLOTS), n_over, ALU.is_gt, ALU.add))
            link(v.memset(zeros32, 0.0))
            link(v.tensor_tensor_scan(cum, n_over, zeros32, 0.0, ALU.add, ALU.add))
            link(v.tensor_scalar(le, cum, over_idx, None, ALU.is_le))
            link(v.tensor_reduce(items[:, 0:1], le, AX.X, ALU.add))
            link(v.tensor_tensor(le, le, cum, ALU.mult))
            link(v.tensor_reduce(items[:, 2:3], le, AX.X, ALU.max))
            link(v.tensor_tensor(items[:, 0:1], items[:, 0:1], first_expert, ALU.add))
            link(v.tensor_scalar(items[:, 0:1], items[:, 0:1], float(NE - 1), None, ALU.min))
            link(v.tensor_tensor(items[:, 1:2], over_idx, items[:, 2:3], ALU.subtract))
            link(v.tensor_scalar(items[:, 1:2], items[:, 1:2], 1.0, is_over, ALU.add, ALU.mult))
            v.tensor_scalar(items[:, 1:2], items[:, 1:2], 0.0, float(S // SLOTS - 1), ALU.max,
                            ALU.min).then_inc(items_ready, 1)
            dve.wait_ge(items_mm, 1)
            v.tensor_copy(table[0:1, 0:TAB], psum[0:1, 0, 0:TAB])
            v.tensor_scalar(table[0:1, TAB:2 * TAB], psum[0:1, 0, P:P + TAB], float(SLOTS), None, ALU.mult)
            v.tensor_scalar(table[0:1, 2 * TAB:2 * TAB + 1], cum[0:1, NE - 1:NE], float(NE), None,
                            ALU.add).then_inc(table_ready, 1)
            dve.wait_ge(table_ready, 1)
            dve.wait_ge(router_exp, 1)
            link(v.reciprocal(r_den, r_den))
            link(v.tensor_tensor(r_gate, r_gate, bc(r_den.unsqueeze(2), [P, NT, TOP_K]), ALU.mult))
            for r in range(NT):
                last = v.tensor_tensor(choice_g[:, r], choice[:, r], bc(r_gate[:, r, :].unsqueeze(2), [P, TOP_K, NE]),
                                       ALU.mult)
            link(last)
            for r in range(NT):
                last = v.tensor_reduce(gates[:, r, :], choice_g[:, r].rearrange("p k e -> p e k"), AX.X, ALU.add)
            link(last)
            dve.wait_ge(padded_zero, 1)

            n_items = dve.value_load(table[0:1, 2 * TAB:2 * TAB + 1], min_val=NE, max_val=MAX_ITEMS)
            with dve.Fori(0, n_items) as i:
                e_next = dve.value_load(table[0:1, bass.ds(i + 1, 1)], min_val=0, max_val=NE - 1)
                s0_next = dve.value_load(table[0:1, bass.ds(i + (TAB + 1), 1)], min_val=0, max_val=S - SLOTS)
                dve.wait_ge(gather_mm, i + 1)
                for r in range(NT):
                    last = v.tensor_scalar(pick[:, r, :], iota[:, bass.ds(s0_next, SLOTS)],
                                           pos[:, r, bass.ds(e_next, 1)], None, ALU.is_equal)
                last.then_inc(pick_ready, 1)
                e = dve.value_load(table[0:1, bass.ds(i, 1)], min_val=0, max_val=NE - 1)
                s0 = dve.value_load(table[0:1, bass.ds(i + TAB, 1)], min_val=0, max_val=S - SLOTS)
                dve.wait_ge(y_mm, i + 1)
                for r in range(NT):
                    v.tensor_scalar(padded[:, r, SLOTS:2 * SLOTS], iota[:, bass.ds(s0, SLOTS)],
                                    pos[:, r, bass.ds(e, 1)], gates[:, r, bass.ds(e, 1)], ALU.is_equal, ALU.mult)
                v.tensor_copy(which_expert, bc(ident[:, bass.ds(e, 1)], [P, SLOTS])).then_inc(padded_ready, 1)
                dve.wait_ge(w_used[MOE_SLOT[3]], i + (PRE_USES[MOE_SLOT[3]] + 1))
                v.tensor_scalar(gate_sb, psum[:, 0, :], LIMIT, None, ALU.min).then_inc(gate_ready, 1)
                v.tensor_scalar(lin_sb, psum[:, 1, :], LIMIT, -LIMIT, ALU.min, ALU.max).then_inc(moe_dve, 1)
                dve.wait_ge(moe_dve, i * 2 + 1)
                v.scalar_tensor_tensor(lin_sb, lin_sb, 1.0, gate_sb, ALU.add, ALU.mult).then_inc(moe_dve, 1)
                dve.wait_ge(moe_dve, i * 2 + 2)
                dve.wait_ge(sigm_ready, i + 1)
                v.tensor_tensor(act_sb, lin_sb, sig_sb, ALU.mult).then_inc(act_ready, 1)

            dve.wait_ge(final_gain_in, 16)
            for r in range(NT):
                dve.wait_ge(final_rs, r + 1)
                v.scalar_tensor_tensor(xr[:, r, :], banks(4 + 2 * r, 6 + 2 * r), rs[:, r:r + 1], vb_region[:, :],
                                       ALU.mult, ALU.mult).then_inc(out_ready, 1)

        @block.gpsimd
        def _(pool):
            g = nc.gpsimd
            steps = [0]

            def root(dst, src, width, n, done):
                g.tensor_scalar(src, src, 1.0 / width, EPS, ALU.mult, ALU.add).then_inc(pool_step, 1)
                steps[0] += 1
                pool.wait_ge(pool_step, steps[0])
                g.tensor_tensor(dst, src, minus_half.broadcast_to([P, n]), ALU.pow).then_inc(done, 1)

            g.memset(idx_region[:, 512:1536], 0.0).then_inc(blocks_zero, 1)
            g.memset(qk_region[:, 1024:3072], 0.0).then_inc(blocks_zero, 1)
            pool.wait_ge(consts_in, 32)
            for r in range(NT):
                pool.wait_ge(squares, r + 1)
                root(rs[:, r:r + 1], ss[:, r:r + 1], D, 1, rs_ready)
            pool.wait_ge(bias_in, 32)
            for n, (sc, bias, keys) in enumerate(((score1, bias1, S), (score0, bias0, P))):
                pool.wait_ge(masks_ready, n + 1)
                g.tensor_tensor(bias, bias, sc.unsqueeze(1).broadcast_to([P, AH, keys]), ALU.add).then_inc(bias_ready, 1)
            pool.wait_ge(ya_mm, 1)
            g.memset(bias_region[:, :], 0.0).then_inc(moe_bias_zero, 1)
            pool.wait_ge(o_squares, 1)
            root(o_rs, o_ss, BD, NT * BH, o_rs_ready)
            pool.wait_ge(merge_mm, NJ)
            g.memset(padded, 0.0).then_inc(padded_zero, 1)
            g.memset(y_sb, 0.0).then_inc(y_ready, 1)
            g.memset(combT_sb, 0.0).then_inc(combT_ready, 1)
            for r in range(NT):
                pool.wait_ge(squares, NT + r + 1)
                root(rs[:, r:r + 1], ss[:, r:r + 1], D, 1, rs_ready)
            for r in range(NT):
                pool.wait_ge(final_ss, r + 1)
                root(rs[:, r:r + 1], ss[:, r:r + 1], D, 1, final_rs)


INPUTS = ["x", "w_in", "w_up_a", "w_up_b", "w_out", "norm_mix", "norm_ffn", "norm_final", "hgrn_norm",
          "lb_logits", "rel_bias", "w_router", "b_router", "w_gu", "b_gu", "w_down", "b_down"]


def kernel(**inputs):
    import concourse.bacc as bacc
    from concourse.bass_utils import run_bass_kernel_spmd as run

    nc = bacc.Bacc("TRN2", target_bir_lowering=False, num_devices=1)
    arrays = {f"in_{n}": np.ascontiguousarray(inputs[n]) for n in INPUTS}
    arrays["in_lb_logits"] = np.ascontiguousarray(
        inputs["lb_logits"].reshape(2, BH, P).transpose(2, 0, 1).reshape(P, 2 * BH))
    arrays["in_hgrn_norm"] = np.ascontiguousarray(inputs["hgrn_norm"][0].T)
    for name, a in zip(("consts", "levels", "onehot"), shape_constants()):
        arrays[f"in_{name}"] = a
    args = [nc.dram_tensor(n, a.shape, mybir.dt.from_np(a.dtype), kind="ExternalInput").ap()
            for n, a in arrays.items()]
    out = nc.dram_tensor("out_y", inputs["x"].shape, F32, kind="ExternalOutput").ap()
    build(nc, *args, out)
    return run(nc, [arrays], core_ids=[0]).results[0]["out_y"]
```

```python
import math
from contextlib import ExitStack

import numpy as np
import concourse.bass as bass
from concourse import mybir

F32 = mybir.dt.float32
F32R = mybir.dt.float32r
I32 = mybir.dt.int32
U32 = mybir.dt.uint32
ALU = mybir.AluOpType
ACT = mybir.ActivationFunctionType
AX = mybir.AxisListType

P = 128
D, S = 1024, 256
NT = S // P
NJ = D // P
AH, AD = 8, 64
IH, ID = 8, 32
TOPK = min(256, S // 4)
BH, BD = 4, 128
NE, TOP_K, FF = 32, 4, 1024
BUCKETS, MAX_DIST = 32, 128
EPS = 1e-6
LIMIT, ALPHA = 7.0, 1.702
SLOTS = 64
MAX_ITEMS = NE + S * TOP_K // SLOTS
TAB = 64
NONCAUSAL = -3.0e38
TAKEN = -3.3e38
DROPPED = -1.0e30
PITCH = S + P - 1

IN_COLS = {"iq": 1536, "aq": 0, "ak": 512, "av": 1024, "bq": 1832, "bf": 2344, "bi": 2856,
           "bg": 3368, "ga0": 3880, "ga1": 4392, "gb0": 4904, "gb1": 5416}
ORDER = ["iq", "aq", "ak", "av", "bq", "bf", "bi", "bg", "ga0", "ga1", "gb0", "gb1"]
IDX_W = IH * ID + IH + ID
RING = 6
CHUNK = 4096
N_PRE = len(ORDER) + 4
RAW = 3
POOL_COLS = 2560
LEVELS = 7


def slot_of(chunk):
    return chunk % RAW if chunk < N_PRE - 1 else RING - 1


def high_slot(chunk):
    return RAW + chunk % RAW


PRE_LOADS = [sum(slot_of(n) == s for n in range(N_PRE)) for s in range(RING)]
USED_BEFORE = [PRE_LOADS[s] if s < RAW else 0 for s in range(RING)]
MOE_SLOT = [0, 3, 1, 4, 2, 5]


def t5_bucket(dist):
    exact = BUCKETS // 2
    if dist < exact:
        return max(dist, 0)
    return min(exact + int(math.log(dist / exact) / math.log(MAX_DIST / exact) * (BUCKETS - exact)),
               BUCKETS - 1)


def shape_constants():
    i = np.arange(P)
    cols = np.zeros((P, 4), np.float32)
    cols[:, 0] = i - NE
    cols[:, 1] = np.where(i < NE, i, 0)
    cols[:, 2] = i >= NE
    cols[:, 3] = -0.5
    consts = np.concatenate([
        np.eye(P), i[:, None] < i[None, :], np.ones((P, P)),
        np.where(i[None, :] <= i[:, None], 0.0, NONCAUSAL),
        np.broadcast_to(np.arange(S), (P, S)), cols], axis=1).astype(np.float32)
    levels = np.zeros((P, LEVELS, P // 2), np.int32)
    for l in range(LEVELS):
        size = 1 << l
        odd = i[(i // size) % 2 == 1]
        levels[:, l, :] = ((i[:, None] // (2 * size) == odd[None, :] // (2 * size))
                           & ((i[:, None] // size) % 2 == 0))
    onehot = np.zeros((BUCKETS, PITCH + 1), np.float32)
    for c in range(PITCH):
        onehot[t5_bucket(S - 1 - c), c] = 1.0
    return consts, levels.reshape(P, LEVELS * P // 2), onehot


def build(nc, x, w_in, w_up_a, w_up_b, w_out, norm_mix, norm_ffn, norm_final, hgrn_norm, lb_logits,
          rel_bias, w_router, b_router, w_gu, b_gu, w_down, b_down, consts, levels, onehot, out):
    ctx = ExitStack()
    with ctx:
        def sb(name, words, dt=F32, parts=P):
            return ctx.enter_context(nc.sbuf_tensor(name, [parts, words], dt))

        def sem(name):
            return ctx.enter_context(nc.semaphore(name))

        with ExitStack() as views:
            def rounded(name, words):
                return views.enter_context(nc.sbuf_tensor(name, [P, words], F32R))

            slot_r = [rounded(f"slot_r{s}", CHUNK) for s in range(RING)]
            x_r, hT_r, hg_r, qk_r, idx_r, work_r = (rounded(name, words) for name, words in (
                ("x_r", NT * D), ("hT_r", NJ * S), ("hg_r", 4096), ("qk_r", 3072), ("idx_r", 1536),
                ("work_r", NT * D)))

        ring = ctx.enter_context(nc.sbuf_tensor("ring", [P, RING, CHUNK], F32))
        x_sb = sb("x_sb", NT * D)
        hT_region = sb("hT_region", NJ * S)
        hg = sb("hg", 4096)
        qk_region = sb("qk_region", 3072)
        idx_region = sb("idx_region", 1536)
        work = sb("work", NT * D)
        work0 = sb("work0", AH * P)
        va_region = sb("va_region", NT * 512)
        score = sb("score", S + P)
        vb_region = sb("vb_region", NT * 512)
        silu_g = sb("silu_g", BH * S)
        sig_a = sb("sig_a", NJ * S)
        sig_b = sb("sig_b", NJ * S)
        bias_region = sb("bias_region", 3072)
        wr_sb = sb("wr_sb", NJ * NE)
        cst = sb("cst", 4 * P + S + 4)
        lvl = sb("lvl", LEVELS * P // 2, I32)
        tiny = sb("tiny", 576)
        itiny = sb("itiny", 8 * NT, U32)
        table = score[0:1, 0:2 * TAB + 1].bitcast(I32)
        psum = ctx.enter_context(nc.psum_tensor("psum", [P, 8, 512], F32))
        rel_rows = nc.dram_tensor("rel_rows", (AH, P, PITCH + 1), F32)

        def banks(a, b):
            return psum[:, a:b, :].rearrange("p b n -> p (b n)")

        ident, before, ones, noncausal = (cst[:, i * P:(i + 1) * P] for i in range(4))
        iota = cst[:, 4 * P:4 * P + S]
        over_idx, first_expert, is_over, minus_half = (
            cst[:, 4 * P + S + i:4 * P + S + i + 1] for i in range(4))

        xr = x_sb[:, :].rearrange("p (r d) -> p r d", r=NT)
        hT = hg[:, 0:2048].rearrange("p (j t) -> p j t", j=NJ)
        hT_high = hT_r[:, :].rearrange("p (j t) -> p j t", j=NJ)
        hT_low = x_r[:, :].rearrange("p (j t) -> p j t", j=NJ)
        x_high, x_low, ident_r = work_r[:, :], x_r[:, :], idx_r[:, 1024:1024 + P]
        mergedT = hT_region[:, :].rearrange("p (j t) -> p j t", j=NJ)
        perm = work[:, :].rearrange("p (r j q) -> p r j q", r=NT, j=NJ)
        relu1 = work[:, :].rearrange("p (h s) -> p h s", h=AH)
        relu0 = work0[:, :].rearrange("p (h s) -> p h s", h=AH)
        probs = {0: relu0, 1: relu1}
        qT = qk_region[:, 0:1024].rearrange("p (m t) -> p m t", m=4)
        kblk = qk_region[:, 1024:3072].rearrange("p (m a t) -> p m a t", m=4, a=2)
        mixT = qk_region[:, 0:1024].rearrange("p (g t) -> p g t", t=P)
        crossT = qk_region[:, 1024:1536].rearrange("p (h t) -> p h t", h=BH)
        y_a_high, y_a_low = qk_r[:, 2048:3072], idx_r[:, 0:1024]
        v_a = va_region[:, :].rearrange("p (r c) -> p r c", r=NT)
        iqT = idx_region[:, 0:512].rearrange("p (m t) -> p m t", m=2)
        ikblk = idx_region[:, 512:1536].rearrange("p (g t) -> p g t", g=4)
        score1, score0 = score[:, 0:S], score[:, S:S + P]
        hq, hk, hf, hprod = (hg[:, i * 1024:(i + 1) * 1024] for i in range(4))
        y_b_high, y_b_low = hg_r[:, 0:1024], hg_r[:, 1024:2048]
        v_b = vb_region[:, :].rearrange("p (r c) -> p r c", r=NT)
        bias1 = bias_region[:, 0:2048].rearrange("p (h s) -> p h s", h=AH)
        bias0 = bias_region[:, 2048:3072].rearrange("p (h s) -> p h s", h=AH)
        pT0 = bias_region[:, 0:2048].rearrange("p (h q) -> p h q", h=AH)
        pT1 = bias_region[:, 2048:3072].rearrange("p (h q) -> p h q", h=AH)
        bias_gu, bias_dn = bias_region[:, 0:2048], bias_region[:, 2048:3072]
        oh_dist = hprod[0:BUCKETS, 0:PITCH + 1]
        rel_sb = hprod[0:BUCKETS, 512:512 + AH]
        rel_row = hprod[0:AH, 576:576 + PITCH + 1]
        gate_sb, lin_sb, sig_sb, act_sb, actT_sb, y_sb, combT_sb, xgT_sb = (
            hg[:, i * 512:(i + 1) * 512] for i in range(8))
        pick = idx_region[:, 0:128].rearrange("p (r s) -> p r s", r=NT)
        padded = idx_region[:, 128:512].rearrange("p (r s) -> p r s", r=NT)
        which_expert = idx_region[:, 512:576]
        h2 = perm
        h2T = mergedT

        at = [0]

        def take(n):
            at[0] += n
            return tiny[:, at[0] - n:at[0]]

        g_mix, ss, rs, ms = take(NJ), take(NT), take(NT), take(2 * NT)
        lb0, lb1, lbm, lb, lb_rest = (take(BH) for _ in range(5))
        tiny_lb = tiny[:, at[0] - 5 * BH:at[0] - 3 * BH]
        g_hgrn = take(BH)
        w_idx = take(NT * IH).rearrange("p (r h) -> p r h", r=NT)
        top8 = take(8)
        row_max, den = {r: take(AH) for r in range(NT)}, {r: take(AH) for r in range(NT)}
        o_ss, o_rs = take(NT * BH), take(NT * BH)
        router_b = take(NE)
        r_logits = take(NT * NE).rearrange("p (r e) -> p r e", r=NT)
        r_top = take(NT * 8).rearrange("p (r k) -> p r k", r=NT)
        r_idx = take(NT * 8).rearrange("p (r k) -> p r k", r=NT)
        r_neg, r_den = take(NT), take(NT)
        r_gate = take(NT * TOP_K).rearrange("p (r k) -> p r k", r=NT)
        sel_pad = take((NT + 1) * NE)
        sel = sel_pad[:, 0:NT * NE].rearrange("p (r e) -> p r e", r=NT)
        gates = take(NT * NE).rearrange("p (r e) -> p r e", r=NT)
        pos = take(NT * NE).rearrange("p (r e) -> p r e", r=NT)
        n_over, cum, le, items = take(NE), take(NE), take(NE), take(4)
        choice = work0[:, 0:256].rearrange("p (r k e) -> p r k e", r=NT, k=TOP_K)
        choice_g = work0[:, 256:512].rearrange("p (r k e) -> p r k e", r=NT, k=TOP_K)
        merge_a, merge_b = work0[:, 0:256], work0[:, 256:512]

        x_in = [sem("x_in0"), sem("x_in1")]
        consts_in, gain_in, params_in, rel_in, cell_zero = (
            sem("consts_in"), sem("gain_in"), sem("params_in"), sem("rel_in"), sem("cell_zero"))
        rel_stored, bias_in = sem("rel_stored"), sem("bias_in")
        w_loaded = [sem(f"w_loaded{s}") for s in range(RING)]
        w_used = [sem(f"w_used{s}") for s in range(RING)]
        squares, rs_ready, pool_step = sem("squares"), sem("rs_ready"), sem("pool_step")
        xn_ready, xT_done, hT_ready = sem("xn_ready"), sem("xT_done"), sem("hT_ready")
        hT_high_ready, hT_low_ready, x_back = sem("hT_high_ready"), sem("hT_low_ready"), sem("x_back")
        x_high_ready, x_low_ready = sem("x_high_ready"), sem("x_low_ready")
        high_ready, low_pool, low_dve = sem("high_ready"), sem("low_pool"), sem("low_dve")
        y_a_low_ready, y_b_high_ready, y_b_low_ready = (
            sem("y_a_low_ready"), sem("y_b_high_ready"), sem("y_b_low_ready"))
        blocks_zero = sem("blocks_zero")
        evacuated = [sem("evacuated0"), sem("evacuated1")]
        rel_done, rel_row_ready = sem("rel_done"), sem("rel_row_ready")
        sig_ready = sem("sig_ready")
        score_mm, relu_ready, masks_ready, bias_ready = (
            sem("score_mm"), sem("relu_ready"), sem("masks_ready"), sem("bias_ready"))
        logits_mm, logits_ready, max_ready, exp_ready, probs_ready = (
            sem("logits_mm"), sem("logits_ready"), sem("max_ready"), sem("exp_ready"), sem("probs_ready"))
        probsT_mm, probsT_ready, ya_mm, ya_ready = (
            sem("probsT_mm"), sem("probsT_ready"), sem("ya_mm"), sem("ya_ready"))
        lb_shifted, lb_exp, dve_step = sem("lb_shifted"), sem("lb_exp"), sem("dve_step")
        hgrn_ready, diag_mm, level_ready, level_mm, mix_ready = (
            sem("hgrn_ready"), sem("diag_mm"), sem("level_ready"), sem("level_mm"), sem("mix_ready"))
        o_mm, o_squared, o_squares, o_rs_ready, o_normed, yb_mm, yb_ready = (
            sem(n) for n in ("o_mm", "o_squared", "o_squares", "o_rs_ready", "o_normed",
                             "yb_mm", "yb_ready"))
        merge_mm, merge_ready, out_mm = sem("merge_mm"), sem("merge_ready"), sem("out_mm")
        ffn_gain_in, moe_bias_zero, moe_bias_in, final_gain_in = (
            sem(n) for n in ("ffn_gain_in", "moe_bias_zero", "moe_bias_in", "final_gain_in"))
        h2T_ready = [sem("h2T_ready0"), sem("h2T_ready1")]
        h2_ready, h2T_mm, router_mm, router_max, router_exp, sel_ready, pos_mm = (
            sem(n) for n in ("h2_ready", "h2T_mm", "router_mm", "router_max",
                             "router_exp", "sel_ready", "pos_mm"))
        items_ready, items_mm, table_ready, n_items_ready, padded_zero = (
            sem(n) for n in ("items_ready", "items_mm", "table_ready", "n_items_ready", "padded_zero"))
        pick_ready, padded_ready, gate_ready, act_ready = (
            sem(n) for n in ("pick_ready", "padded_ready", "gate_ready", "act_ready"))
        sigm_ready, xg_ready, actT_ready, combT_ready, y_ready = (
            sem(n) for n in ("sigm_ready", "xg_ready", "actT_ready", "combT_ready", "y_ready"))
        gather_mm, actT_mm, combT_mm, y_mm, all_mm = (
            sem(n) for n in ("gather_mm", "actT_mm", "combT_mm", "y_mm", "all_mm"))
        moe_dve = sem("moe_dve")
        final_ss, final_rs, out_ready, out_stored = (
            sem(n) for n in ("final_ss", "final_rs", "out_ready", "out_stored"))

        w_in_v = w_in[0].rearrange("(p j) n -> p j n", j=NJ)
        up_v = [w[0].rearrange("(m p) n -> p m n", p=P) for w in (w_up_a, w_up_b)]
        out_v = w_out[0].rearrange("(m p) n -> p m n", p=P)
        gu_v = w_gu[0].rearrange("e (p j) n -> e p j n", j=NJ)
        down_v = w_down[0].rearrange("e (m p) n -> e p m n", p=P)

        def slot_in(n):
            w = IDX_W if n == 0 else 512
            return ring[:, slot_of(n), 0:NJ * w].rearrange("p (j n) -> p j n", j=NJ)

        def split_parts(n, form):
            return [slot_r[s][:, :].rearrange(form[0], **form[1]) for s in (high_slot(n), slot_of(n))]

        IN_FORM = ("p (j n) -> p j n", {"j": NJ})
        UP_FORM = ("p (m n) -> p m n", {"m": 4})

        def slot4(s):
            return ring[:, s, :].rearrange("p (m n) -> p m n", m=4)

        def slot_gu(c):
            return ring[:, MOE_SLOT[c], :].rearrange("p (j n) -> p j n", j=2)

        block = ctx.enter_context(nc.Block())

        @block.sync
        def _(sp):
            for r in range(NT):
                sp.dma_start(xr[:, r, :], x[0, r * P:(r + 1) * P, :]).then_inc(x_in[r], 16)
            for n in range(N_PRE):
                s = slot_of(n)
                if n == 1:
                    for dst, src in [
                        (tiny_lb, lb_logits), (g_hgrn, hgrn_norm), (lvl[:, :], levels),
                        (router_b, b_router.partition_broadcast(P).rearrange("p a e -> p (a e)")),
                        (wr_sb[:, :], w_router[0].rearrange("(p j) e -> p (j e)", j=NJ)),
                    ]:
                        sp.dma_start(dst, src).then_inc(params_in, 16)
                    sp.wait_ge(consts_in, 16)
                    sp.wait_ge(gain_in, 16)
                    sp.wait_ge(rel_in, 32)
                    sp.wait_ge(params_in, 80)
                if n == N_PRE - 1:
                    sp.wait_ge(w_used[slot_of(len(ORDER) - 1)], len(ORDER) // RAW)
                elif n >= RAW:
                    sp.wait_ge(w_used[s], n // RAW)
                if n < len(ORDER):
                    c0 = IN_COLS[ORDER[n]]
                    w = IDX_W if n == 0 else 512
                    sp.dma_start(slot_in(n), w_in_v[:, :, c0:c0 + w]).then_inc(w_loaded[s], 16)
                elif n < len(ORDER) + 2:
                    sp.dma_start(slot4(s), up_v[n - len(ORDER)]).then_inc(w_loaded[s], 16)
                else:
                    m0 = 4 * (n - len(ORDER) - 2)
                    sp.dma_start(slot4(s), out_v[:, m0:m0 + 4, :]).then_inc(w_loaded[s], 16)

            def load_item(e, i, first=False):
                for c in range(RING):
                    s = MOE_SLOT[c]
                    if c == RING - 1:
                        if first:
                            sp.wait_ge(out_mm, 2 * NT)
                        else:
                            sp.wait_ge(y_mm, i + 1)
                    elif first:
                        sp.wait_ge(w_used[s % RAW], PRE_LOADS[s % RAW])
                    else:
                        sp.wait_ge(w_used[s], i + USED_BEFORE[s])
                    if c < 4:
                        src = gu_v[bass.ds(e, 1), :, 2 * c:2 * c + 2, :].rearrange("e p j n -> (e p) j n")
                        sp.dma_start(slot_gu(c), src).then_inc(w_loaded[s], 16)
                    else:
                        m0 = 4 * (c - 4)
                        src = down_v[bass.ds(e, 1), :, m0:m0 + 4, :].rearrange("e p m n -> (e p) m n")
                        sp.dma_start(slot4(s), src).then_inc(w_loaded[s], 16)

            load_item(0, 0, True)
            sp.wait_ge(table_ready, 1)
            n_items = sp.value_load(table[0:1, 2 * TAB:2 * TAB + 1], min_val=NE, max_val=MAX_ITEMS)
            with sp.Fori(1, n_items) as i:
                e = sp.value_load(table[0:1, bass.ds(i, 1)], min_val=0, max_val=NE - 1)
                load_item(e, i)
            for r in range(NT):
                for half in range(2):
                    cols = slice(half * 512, (half + 1) * 512)
                    sp.wait_ge(out_ready, 2 * r + half + 1)
                    sp.dma_start(out[0, r * P:(r + 1) * P, cols], xr[:, r, cols]).then_inc(out_stored, 16)
            sp.wait_ge(out_stored, 32 * NT)

        @block.tensor
        def _(pe):
            mm = nc.tensor.matmul

            def transposes(src, bank0, done):
                for r in range(NT):
                    pe.wait_ge(*src(r))
                    dst = banks(bank0 + 2 * r, bank0 + 2 * r + 2).rearrange("p (j t) -> p j t", j=NJ)
                    for j in range(NJ):
                        last = nc.tensor.transpose(dst[:, j, :], perm[:, r, j, :], ident)
                    last.then_inc(done, 1)

            def low_part(n):
                pe.wait_ge(low_pool, n)
                pe.wait_ge(low_dve, n)

            def keep_warm(n, bank):
                for _ in range(n):
                    mm(psum[:, bank, 0:P], ident, ident, start=True, stop=True, skip_group_check=True)

            def half_T(n, half):
                (high, low), b = split_parts(n, IN_FORM), 2 * (n % 2) + half
                for c in range(2):
                    dst = psum[:, b, c * S:(c + 1) * S]
                    cols = slice((2 * half + c) * P, (2 * half + c + 1) * P)
                    for j in range(NJ):
                        mm(dst, high[:, j, cols], hT_high[:, j, :], start=(j == 0), stop=False)
                        mm(dst, high[:, j, cols], hT_low[:, j, :], start=False, stop=False)
                    if half == 0 and c == 0:
                        low_part(n)
                    for j in range(NJ):
                        last = mm(dst, low[:, j, cols], hT_high[:, j, :], start=False, stop=(j == NJ - 1))
                return last

            def half_tok(n, half):
                (high, low), b = split_parts(n, IN_FORM), 2 * (n % 2) + half
                rows = slice(half * P, (half + 1) * P)
                for j in range(NJ):
                    mm(psum[:, b, :], hT_high[:, j, rows], high[:, j, :], start=(j == 0), stop=False)
                    mm(psum[:, b, :], hT_low[:, j, rows], high[:, j, :], start=False, stop=False)
                if half == 0:
                    low_part(n)
                for j in range(NJ):
                    last = mm(psum[:, b, :], hT_high[:, j, rows], low[:, j, :], start=False, stop=(j == NJ - 1))
                return last

            def project(n, half):
                if half == 0:
                    pe.wait_ge(high_ready, n)
                    if n >= 2:
                        pe.wait_ge(evacuated[n % 2], n // 2)
                form = half_tok if ORDER[n] in ("av", "bi") else half_T
                last = form(n, half)
                if half:
                    last.then_inc(w_used[slot_of(n)], 1)

            pe.wait_ge(cell_zero, 1)
            for _ in range(3):
                mm(psum[:, 7, :], idx_region[:, 512:640], idx_region[:, 512:1024], start=True, stop=True)
            pe.wait_ge(consts_in, 16)
            transposes(lambda r: (xn_ready, r + 1), 0, xT_done)
            pe.wait_ge(rel_in, 32)
            mm(psum[0:AH, 7, 0:PITCH + 1], rel_sb, oh_dist, start=True, stop=True).then_inc(rel_done, 1)
            pe.wait_ge(hT_ready, NT)

            pe.wait_ge(w_loaded[0], 16)
            w0 = slot_in(0)
            for m in range(2):
                for j in range(NJ):
                    mm(psum[:, 0, m * S:(m + 1) * S], w0[:, j, m * P:(m + 1) * P], hT[:, j, :],
                       start=(j == 0), stop=(j == NJ - 1))
            for j in range(NJ):
                for g in range(4):
                    mm(psum[32 * g:32 * g + 32, 1, 0:S], w0[:, j, IH * ID + IH:IDX_W], hT[:, j, :],
                       start=(j == 0), stop=(j == NJ - 1))
            for r in range(NT):
                for j in range(NJ):
                    last = mm(psum[:, 1, S + r * IH:S + (r + 1) * IH], hT[:, j, r * P:(r + 1) * P],
                              w0[:, j, IH * ID:IH * ID + IH], start=(j == 0), stop=(j == NJ - 1))
            last.then_inc(w_used[0], 1)

            def scores(r):
                keys = (r + 1) * P
                group = 512 // keys
                for m in range(2):
                    for g in range(4 // group):
                        last = mm(psum[:, 4 + m * (4 // group) + g, 0:group * keys], iqT[:, m, r * P:(r + 1) * P],
                                  ikblk[:, g * group:(g + 1) * group, 0:keys], start=True, stop=True)
                last.then_inc(score_mm, 1)

            def logits(r):
                keys = (r + 1) * P
                for m in range(4):
                    dst = banks(4, 8)[:, m * 2 * keys:(m + 1) * 2 * keys]
                    last = mm(dst, qT[:, m, r * P:(r + 1) * P], kblk[:, m, :, 0:keys], start=True, stop=True)
                last.then_inc(logits_mm, 1)

            def probs_T(rnd):
                dst = banks(4, 6).rearrange("p (g q) -> p g q", q=P)
                for g in range(8):
                    src = probs[0][:, g, :] if rnd == 2 else \
                        probs[1][:, 4 * rnd + g // 2, (g % 2) * P:(g % 2 + 1) * P]
                    last = nc.tensor.transpose(dst[:, g, :], src, ident)
                last.then_inc(probsT_mm, 1)

            def values():
                dst = banks(4, 6).rearrange("p (m q) -> p m q", m=4)
                for h in range(AH):
                    rows = slice((h % 2) * AD, (h % 2 + 1) * AD)
                    cols = slice(h * AD, (h + 1) * AD)
                    mm(dst[rows, h // 2, :], v_a[:, 0, cols], pT0[:, h, :], start=True, stop=False)
                    last = mm(dst[rows, h // 2, P:S], v_a[:, 1, cols], pT1[:, h, :], start=False, stop=True)
                last.then_inc(ya_mm, 1)

            def diagonal():
                dst = banks(6, 8).rearrange("p (g t) -> p g t", t=P)
                for g in range(BH * NT):
                    cols = slice(g * P, (g + 1) * P)
                    last = mm(dst[:, g, :], hk[:, cols], hq[:, cols], start=True, stop=True)
                last.then_inc(diag_mm, 1)

            def level(l):
                pe.wait_ge(level_ready, l + 1)
                dst = psum[:, 6 + l % 2, :]
                if l < LEVELS:
                    for g in range(BH * NT):
                        odd = hq[:, g * P:(g + 1) * P].rearrange("p (n a l) -> p a n l", a=2, l=1 << l)[:, 1]
                        last = mm(dst[:, g * 64:(g + 1) * 64], hk[:, g * P:(g + 1) * P], odd, start=True, stop=True)
                else:
                    for h in range(BH):
                        last = mm(dst[:, h * P:(h + 1) * P], hk[:, h * S:h * S + P], hq[:, h * S + P:(h + 1) * S],
                                  start=True, stop=True)
                last.then_inc(level_mm, 1)

            pe.wait_ge(hT_low_ready, NT)
            project(1, 0)
            project(1, 1)
            pe.wait_ge(evacuated[0], 1)
            scores(1)
            project(2, 0)
            project(2, 1)
            pe.wait_ge(relu_ready, 1)
            scores(0)
            for n in (3, 4, 5):
                project(n, 0)
                project(n, 1)
            pe.wait_ge(relu_ready, 2)
            pe.wait_ge(evacuated[1], 1)
            pe.wait_ge(evacuated[0], 2)
            logits(1)
            project(6, 0)
            pe.wait_ge(logits_ready, 1)
            logits(0)
            project(6, 1)
            pe.wait_ge(hgrn_ready, 1)
            diagonal()
            project(7, 0)
            level(0)
            project(7, 1)
            level(1)
            pe.wait_ge(probs_ready, 1)
            pe.wait_ge(logits_ready, 2)
            probs_T(0)
            project(8, 0)
            level(2)
            pe.wait_ge(probsT_ready, 1)
            probs_T(1)
            project(8, 1)
            level(3)
            pe.wait_ge(probs_ready, 2)
            pe.wait_ge(probsT_ready, 2)
            probs_T(2)
            project(9, 0)
            level(4)
            pe.wait_ge(probsT_ready, 3)
            pe.wait_ge(evacuated[1], 2)
            values()
            project(9, 1)
            level(5)
            project(10, 0)
            level(6)
            project(10, 1)
            level(7)
            project(11, 0)
            pe.wait_ge(mix_ready, 1)
            pe.wait_ge(evacuated[0], 4)
            for h in range(BH):
                cols = slice(h * P, (h + 1) * P)
                mm(psum[:, 6, cols], mixT[:, h * NT, :], v_b[:, 0, cols], start=True, stop=True)
                mm(psum[:, 7, cols], crossT[:, h, :], v_b[:, 0, cols], start=True, stop=False)
                last = mm(psum[:, 7, cols], mixT[:, h * NT + 1, :], v_b[:, 1, cols], start=False, stop=True)
            last.then_inc(o_mm, 1)
            project(11, 1)

            def up(n, m, y_high, y_low):
                high, low = split_parts(n, UP_FORM)
                dst = psum[:, m % 4, (n - len(ORDER)) * S:(n - len(ORDER) + 1) * S]
                cols = slice(m * P, (m + 1) * P)
                tok = [slice(k * S, (k + 1) * S) for k in range(4)]
                for k in range(4):
                    mm(dst, high[:, k, cols], y_high[:, tok[k]], start=(k == 0), stop=False)
                    mm(dst, high[:, k, cols], y_low[:, tok[k]], start=False, stop=False)
                for k in range(4):
                    last = mm(dst, low[:, k, cols], y_high[:, tok[k]], start=False, stop=(k == 3))
                return last

            up_a, up_b = len(ORDER), len(ORDER) + 1
            pe.wait_ge(o_normed, 1)
            ob = hq.rearrange("p (r h e) -> p r h e", r=NT, h=BH)
            dst = banks(6, 8).rearrange("p (h t) -> p h t", h=BH)
            for h in range(BH):
                for r in range(NT):
                    last = nc.tensor.transpose(dst[:, h, r * P:(r + 1) * P], ob[:, r, h, :], ident)
            last.then_inc(yb_mm, 1)

            pe.wait_ge(ya_ready, 1)
            pe.wait_ge(y_a_low_ready, 1)
            pe.wait_ge(high_ready, up_a)
            low_part(up_a)
            pe.wait_ge(evacuated[0], len(ORDER) // 2)
            pe.wait_ge(evacuated[1], len(ORDER) // 2)
            for m in range(4):
                up(up_a, m, y_a_high, y_a_low)
            pe.wait_ge(y_b_high_ready, 1)
            pe.wait_ge(y_b_low_ready, 1)
            pe.wait_ge(high_ready, up_b)
            low_part(up_b)
            for m in range(NJ):
                if m >= 4:
                    pe.wait_ge(merge_ready, m - 3)
                    last = up(up_a, m, y_a_high, y_a_low)
                if m == NJ - 1:
                    last.then_inc(w_used[slot_of(up_a)], 1)
                up(up_b, m, y_b_high, y_b_low).then_inc(merge_mm, 1)
            pe.wait_ge(x_high_ready, 2)
            pe.wait_ge(x_low_ready, 1)
            halves = [(r, half) for r in range(NT) for half in range(2)]
            for r, half in halves:
                cols = slice(r * D + half * 512, r * D + (half + 1) * 512)
                first = mm(psum[:, 4 + 2 * r + half, :], ident_r, x_high[:, cols], start=True, stop=False,
                           skip_group_check=True)
                last = mm(psum[:, 4 + 2 * r + half, :], ident_r, x_low[:, cols], start=False, stop=True,
                          skip_group_check=True)
                if (r, half) == halves[0]:
                    first.then_inc(w_used[slot_of(up_b)], 1)
            last.then_inc(y_mm, 1)

            def h2_transposes(r):
                dst = banks(2 * r, 2 * r + 2).rearrange("p (j t) -> p j t", j=NJ)
                for j in range(NJ):
                    if j % 4 == 0:
                        pe.wait_ge(h2_ready, 2 * r + j // 4 + 1)
                    last = nc.tensor.transpose(dst[:, j, :], h2[:, r, j, :], ident)
                last.then_inc(h2T_mm, 1)

            def router(r):
                pe.wait_ge(h2T_ready[r], 2)
                for j in range(NJ):
                    last = mm(psum[:, 2 * r, 0:NE], h2T[:, j, r * P:(r + 1) * P],
                              wr_sb[:, j * NE:(j + 1) * NE], start=(j == 0), stop=(j == NJ - 1))
                last.then_inc(router_mm, 1)

            for r, half in halves:
                for m in range(NJ):
                    s = slot_of(len(ORDER) + 2 + m // 4)
                    if (r, half) == halves[0]:
                        if m % 4 == 0:
                            pe.wait_ge(w_loaded[s], 16 * PRE_LOADS[s])
                        pe.wait_ge(merge_ready, m + 1)
                    last = mm(psum[:, 4 + 2 * r + half, :], mergedT[:, m, r * P:(r + 1) * P],
                              slot4(s)[:, m % 4, half * 512:(half + 1) * 512],
                              start=False, stop=(m == NJ - 1), skip_group_check=True)
                    if (r, half) == halves[-1] and m == 3:
                        last.then_inc(w_used[s], 1)
                last.then_inc(out_mm, 1)
                if (r, half) == halves[-2]:
                    h2_transposes(0)
            router(0)
            keep_warm(2, 1)
            h2_transposes(1)
            keep_warm(3, 1)
            router(1)
            keep_warm(6, 3)
            pe.wait_ge(sel_ready, NT)
            mm(psum[:, 1, 0:3 * NE], before, sel_pad, start=True, stop=False, skip_group_check=True)
            mm(psum[:, 1, NE:3 * NE], ones, sel[:, 0, :].unsqueeze(1).broadcast_to([P, 2, NE]), start=False, stop=False,
               skip_group_check=True)
            mm(psum[:, 1, 2 * NE:3 * NE], ones, sel[:, 1, :], start=False, stop=True,
               skip_group_check=True).then_inc(pos_mm, 1)
            keep_warm(3, 3)

            def gather(part):
                for j in range(4 * part, 4 * part + 4):
                    for r in range(NT):
                        last = mm(psum[:, 3, j * SLOTS:(j + 1) * SLOTS], h2[:, r, j, :], pick[:, r, :],
                                  start=(r == 0), stop=(r == NT - 1))
                return last

            def combine(r, half):
                return mm(psum[:, 4 + 2 * r + half, :], combT_sb[:, (half * NT + r) * P:(half * NT + r + 1) * P],
                          y_sb, start=False, stop=True, skip_group_check=True)

            pe.wait_ge(pick_ready, 1)
            gather(0)
            gather(1).then_inc(gather_mm, 1)
            pe.wait_ge(items_ready, 1)
            mm(psum[0:1, 2, 0:P], items[:, 0:1], ident, start=True, stop=True)
            mm(psum[0:1, 2, P:2 * P], items[:, 1:2], ident, start=True, stop=True).then_inc(items_mm, 1)
            pe.wait_ge(moe_bias_in, 32)
            pe.wait_ge(n_items_ready, 1)
            n_items = pe.value_load(table[0:1, 2 * TAB:2 * TAB + 1], min_val=NE, max_val=MAX_ITEMS)
            with pe.Fori(0, n_items) as i:
                pe.wait_ge(xg_ready, i + 1)
                for c in range(4):
                    s = MOE_SLOT[c]
                    pe.wait_ge(w_loaded[s], (i + PRE_LOADS[s] + 1) * 16)
                    for jj in range(2):
                        j = 2 * c + jj
                        for b in range(2):
                            for half in range(2):
                                c0 = b * FF + half * 512
                                last = mm(psum[half * 64:half * 64 + 64, b, :], xgT_sb[:, j * SLOTS:(j + 1) * SLOTS],
                                          slot_gu(c)[:, jj, c0:c0 + 512], start=(j == 0), stop=(j == NJ - 1),
                                          skip_group_check=True)
                    last.then_inc(w_used[s], 1)
                    if c == 2:
                        pe.wait_ge(padded_ready, i + 1)
                        for b in range(2):
                            for half in range(2):
                                c0 = b * FF + half * 512
                                mm(psum[half * 64:half * 64 + 64, b, :], which_expert, bias_gu[:, c0:c0 + 512],
                                   start=False, stop=False, skip_group_check=True)
                        pe.wait_ge(combT_ready, i + 1)
                        pe.wait_ge(pick_ready, i + 2)
                        gather(0)
                pe.wait_ge(y_ready, i + 1)
                for r, half in halves:
                    combine(r, half)
                pe.wait_ge(act_ready, i + 1)
                for c in range(4):
                    last = nc.tensor.transpose(psum[:, 2, c * P:(c + 1) * P], act_sb[:, c * P:(c + 1) * P], ident)
                last.then_inc(actT_mm, 1)
                gather(1).then_inc(gather_mm, 1)
                pe.wait_ge(actT_ready, i + 1)
                for half in range(2):
                    mm(psum[half * 64:half * 64 + 64, 2, :], which_expert, bias_dn[:, half * 512:(half + 1) * 512],
                       start=True, stop=False, skip_group_check=True)
                for c in range(4, RING):
                    s = MOE_SLOT[c]
                    pe.wait_ge(w_loaded[s], (i + PRE_LOADS[s] + 1) * 16)
                    for k in range(4):
                        m = 4 * (c - 4) + k
                        a = (m % 4) * P + (m // 4) * SLOTS
                        for half in range(2):
                            last = mm(psum[half * 64:half * 64 + 64, 2, :], actT_sb[:, a:a + SLOTS],
                                      slot4(s)[:, k, half * 512:(half + 1) * 512], start=False, stop=(m == NJ - 1),
                                      skip_group_check=True)
                    if c == 4:
                        last.then_inc(w_used[s], 1)
                        pe.wait_ge(xg_ready, i + 2)
                        for q in range(2 * NT):
                            a = (1 - q // NT) * SLOTS
                            tr = nc.tensor.transpose(psum[:, 3, q * P:(q + 1) * P], padded[:, q % NT, a:a + P], ident)
                        tr.then_inc(combT_mm, 1)
                last.then_inc(y_mm, 1)
            pe.wait_ge(y_ready, n_items + 1)
            pe.wait_ge(combT_ready, n_items + 1)
            for r, half in halves:
                combine(r, half).then_inc(all_mm, 1)

        @block.scalar
        def _(act):
            f = nc.scalar.activation
            act.dma_start(cst[:, :], consts).then_inc(consts_in, 16)
            act.dma_start(g_mix, norm_mix[0].rearrange("(p j) -> p j", j=NJ)).then_inc(gain_in, 16)
            act.wait_ge(cell_zero, 1)
            f(row_max[0][:, 1:2], row_max[0][:, 0:1], ACT.Square)
            act.dma_start(oh_dist, onehot).then_inc(rel_in, 16)
            act.dma_start(rel_sb, rel_bias).then_inc(rel_in, 16)
            junk = hT_region[:, 0:D]
            for r in range(NT):
                act.wait_ge(x_in[r], 16)
                f(junk, xr[:, r, :], ACT.Square, accum_out=ss[:, r:r + 1]).then_inc(squares, 1)
                act.wait_ge(squares, r + 1)

            def take_high(n):
                act.wait_ge(w_loaded[slot_of(n)], 16 * (n // RAW + 1))
                f(slot_r[high_slot(n)][:, :], ring[:, slot_of(n), :], ACT.Copy).then_inc(high_ready, 1)

            for r in range(NT):
                act.wait_ge(hT_ready, r + 1)
                cols = slice(r * P, (r + 1) * P)
                f(hT_high[:, :, cols], hT[:, :, cols], ACT.Copy).then_inc(hT_high_ready, 1)
            act.wait_ge(rel_row_ready, 1)
            act.dma_start(rel_rows.ap(), rel_row.unsqueeze(1).broadcast_to([AH, P, PITCH + 1])).then_inc(rel_stored, 16)
            act.wait_ge(lb_shifted, 1)
            f(tiny_lb, tiny_lb, ACT.Exp).then_inc(lb_exp, 1)
            take_high(1)
            act.wait_ge(rel_stored, 16)
            for r, dst in ((1, bias1), (0, bias0)):
                keys = (r + 1) * P
                src = bass.AP(rel_rows, S - 1 - r * P, [[PITCH, P], [P * (PITCH + 1), AH], [1, keys]])
                act.dma_start(dst, src).then_inc(bias_in, 16)

            def chunk_done(n):
                act.wait_ge(w_used[slot_of(n)], n // RAW + 1)

            def proj(n):
                return banks(2 * (n % 2), 2 * (n % 2) + 2)

            take_high(2)
            take_high(3)
            chunk_done(1)
            f(qk_region[:, 0:1024], proj(1), ACT.Copy).then_inc(evacuated[1], 1)
            act.wait_ge(score_mm, 1)
            f(work[:, :], banks(4, 8), ACT.Relu, scale=ID ** -0.5).then_inc(relu_ready, 1)
            take_high(4)
            act.wait_ge(score_mm, 2)
            f(work0[:, :], banks(4, 6), ACT.Relu, scale=ID ** -0.5).then_inc(relu_ready, 1)
            take_high(5)
            chunk_done(3)
            f(va_region[:, :], proj(3), ACT.Copy).then_inc(evacuated[1], 1)
            take_high(6)
            chunk_done(4)
            f(hq, proj(4), ACT.Sigmoid).then_inc(sig_ready, 1)
            take_high(7)
            chunk_done(5)
            f(hf, proj(5), ACT.Sigmoid).then_inc(evacuated[1], 1)
            for n, r in enumerate((1, 0)):
                act.wait_ge(max_ready, n + 1)
                for h in range(AH):
                    last = f(probs[r][:, h, :], probs[r][:, h, :], ACT.Exp, bias=row_max[r][:, h:h + 1],
                             accum_out=den[r][:, h:h + 1])
                last.then_inc(exp_ready, 1)
            take_high(8)
            chunk_done(6)
            f(vb_region[:, :], proj(6), ACT.Copy).then_inc(evacuated[0], 1)
            take_high(9)
            chunk_done(7)
            f(silu_g[:, :], proj(7), ACT.Sigmoid).then_inc(sig_ready, 1)
            for rnd in range(2):
                act.wait_ge(probsT_mm, rnd + 1)
                src = banks(4, 6).rearrange("p (h s q) -> p h s q", h=4, s=2)
                f(pT0[:, 4 * rnd:4 * rnd + 4, P:S], src[:, :, 0, :], ACT.Copy)
                f(pT1[:, 4 * rnd:4 * rnd + 4, :], src[:, :, 1, :], ACT.Copy).then_inc(probsT_ready, 1)
            take_high(10)
            chunk_done(8)
            f(sig_a[:, 0:1024], proj(8), ACT.Sigmoid).then_inc(evacuated[0], 1)
            act.wait_ge(probsT_mm, 3)
            f(pT0[:, :, 0:P], banks(4, 6).rearrange("p (h q) -> p h q", h=AH), ACT.Copy).then_inc(probsT_ready, 1)
            act.wait_ge(ya_mm, 1)
            f(y_a_high, banks(4, 6), ACT.Copy).then_inc(ya_ready, 1)
            act.dma_start(va_region[:, :], norm_ffn[0].partition_broadcast(P)).then_inc(ffn_gain_in, 16)
            take_high(11)
            chunk_done(9)
            f(sig_a[:, 1024:2048], proj(9), ACT.Sigmoid).then_inc(evacuated[1], 1)
            act.wait_ge(moe_bias_zero, 1)
            act.dma_start(bias_gu[0:NE, :], b_gu[0]).then_inc(moe_bias_in, 16)
            act.dma_start(bias_dn[0:NE, :], b_down[0]).then_inc(moe_bias_in, 16)
            take_high(12)
            chunk_done(10)
            f(sig_b[:, 0:1024], proj(10), ACT.Sigmoid).then_inc(evacuated[0], 1)
            act.wait_ge(o_mm, 1)
            f(hk, banks(6, 8), ACT.Square).then_inc(o_squared, 1)
            act.dma_start(vb_region[:, :], norm_final.partition_broadcast(P)).then_inc(final_gain_in, 16)
            take_high(13)
            chunk_done(11)
            f(sig_b[:, 1024:2048], proj(11), ACT.Sigmoid).then_inc(evacuated[1], 1)
            for r in range(NT):
                act.dma_start(xr[:, r, :], x[0, r * P:(r + 1) * P, :]).then_inc(x_back, 16)
            act.wait_ge(yb_ready, 1)
            f(y_b_high, hf, ACT.Copy).then_inc(y_b_high_ready, 1)
            f(ident_r, ident, ACT.Copy).then_inc(x_high_ready, 1)
            act.wait_ge(x_back, 32)
            f(x_high, x_sb[:, :], ACT.Copy).then_inc(x_high_ready, 1)

            def copy_h2T(r):
                act.wait_ge(h2T_mm, r + 1)
                f(h2T[:, 4:8, r * P:(r + 1) * P], psum[:, 2 * r + 1, :].rearrange("p (j t) -> p j t", j=4),
                  ACT.Copy).then_inc(h2T_ready[r], 1)

            for n in range(2 * NT):
                if n == 2 * NT - 1:
                    copy_h2T(0)
                act.wait_ge(out_mm, n + 1)
                f(sig_a[:, n * 512:(n + 1) * 512], psum[:, 4 + n, :], ACT.Square, scale=D ** -0.5,
                  accum_out=ms[:, n:n + 1]).then_inc(squares, 1)
            copy_h2T(1)
            act.wait_ge(router_max, NT)
            for r in range(NT):
                last = f(r_gate[:, r, :], r_top[:, r, 0:TOP_K], ACT.Exp, bias=r_neg[:, r:r + 1],
                         accum_out=r_den[:, r:r + 1])
            last.then_inc(router_exp, 1)
            act.wait_ge(gather_mm, 1)
            f(xgT_sb, psum[:, 3, :], ACT.Copy).then_inc(xg_ready, 1)
            act.wait_ge(n_items_ready, 1)
            n_items = act.value_load(table[0:1, 2 * TAB:2 * TAB + 1], min_val=NE, max_val=MAX_ITEMS)
            with act.Fori(0, n_items) as i:
                act.wait_ge(gate_ready, i + 1)
                f(sig_sb, gate_sb, ACT.Sigmoid, scale=ALPHA).then_inc(sigm_ready, 1)
                act.wait_ge(actT_mm, i + 1)
                f(actT_sb, psum[:, 2, :], ACT.Copy).then_inc(actT_ready, 1)
                act.wait_ge(gather_mm, i + 2)
                f(xgT_sb, psum[:, 3, :], ACT.Copy).then_inc(xg_ready, 1)
                act.wait_ge(combT_mm, i + 1)
                f(combT_sb, psum[:, 3, :], ACT.Copy).then_inc(combT_ready, 1)
                act.wait_ge(y_mm, i + 2)
                f(y_sb, psum[:, 2, :], ACT.Copy).then_inc(y_ready, 1)
            for n in range(2 * NT):
                act.wait_ge(all_mm, n + 1)
                f(sig_a[:, n * 512:(n + 1) * 512], psum[:, 4 + n, :], ACT.Square, scale=D ** -0.5,
                  accum_out=ms[:, n:n + 1]).then_inc(final_ss, 1)

        @block.vector
        def _(dve):
            v = nc.vector
            steps = [0]

            def link(ins):
                steps[0] += 1
                ins.then_inc(dve_step, 1)
                dve.wait_ge(dve_step, steps[0])

            def bc(ap, shape):
                return ap.broadcast_to(shape)

            for r in range(NT):
                dve.wait_ge(rs_ready, r + 1)
                v.tensor_scalar(perm[:, r], xr[:, r, :].rearrange("p (q j) -> p j q", j=NJ), rs[:, r:r + 1], None,
                                ALU.mult).then_inc(xn_ready, 1)
            dve.wait_ge(gain_in, 16)
            for r in range(NT):
                dve.wait_ge(xT_done, r + 1)
                v.tensor_tensor(hT[:, :, r * P:(r + 1) * P], banks(2 * r, 2 * r + 2).rearrange("p (j t) -> p j t", j=NJ),
                                bc(g_mix.unsqueeze(2), [P, NJ, P]), ALU.mult).then_inc(hT_ready, 1)
            dve.wait_ge(rel_done, 1)
            v.tensor_copy(rel_row, psum[0:AH, 7, 0:PITCH + 1]).then_inc(rel_row_ready, 1)
            dve.wait_ge(params_in, 80)
            link(v.tensor_tensor(lbm, lb0, lb1, ALU.max))
            v.tensor_tensor(lb0, lb0, lbm, ALU.subtract)
            v.tensor_tensor(lb1, lb1, lbm, ALU.subtract).then_inc(lb_shifted, 1)
            for r in range(NT):
                dve.wait_ge(hT_high_ready, r + 1)
                cols = slice(r * P, (r + 1) * P)
                v.tensor_tensor(hT_low[:, :, cols], hT[:, :, cols], hT_high[:, :, cols].bitcast(F32),
                                ALU.subtract).then_inc(hT_low_ready, 1)

            def take_low(n):
                dve.wait_ge(high_ready, n)
                cols = slice(POOL_COLS, CHUNK)
                v.tensor_tensor(slot_r[slot_of(n)][:, cols], ring[:, slot_of(n), cols],
                                slot_r[high_slot(n)][:, cols].bitcast(F32), ALU.subtract).then_inc(low_dve, 1)

            take_low(1)
            dve.wait_ge(lb_exp, 1)
            link(v.tensor_tensor(lbm, lb0, lb1, ALU.add))
            link(v.reciprocal(lbm, lbm))
            link(v.tensor_tensor(lb, lb0, lbm, ALU.mult))
            v.tensor_scalar(lb_rest, lb, -1.0, 1.0, ALU.mult, ALU.add)

            def chunk_done(n):
                dve.wait_ge(w_used[slot_of(n)], n // RAW + 1)

            def proj(n):
                return banks(2 * (n % 2), 2 * (n % 2) + 2)

            chunk_done(0)
            dve.wait_ge(blocks_zero, 2)
            v.tensor_copy(idx_region[:, 0:512], psum[:, 0, :])
            for g in range(4):
                rows = slice(32 * g, 32 * g + 32)
                v.tensor_copy(ikblk[rows, g, :], psum[rows, 1, 0:S])
            v.tensor_scalar(w_idx, psum[:, 1, S:S + NT * IH].rearrange("p (r h) -> p r h", r=NT), IH ** -0.5, None,
                            ALU.mult).then_inc(evacuated[0], 1)
            dve.wait_ge(evacuated[0], 1)

            def top_keys(n, r, sc, relu):
                dve.wait_ge(relu_ready, n)
                link(v.tensor_scalar(sc, relu[:, 0, :], w_idx[:, r, 0:1], None, ALU.mult))
                for h in range(1, IH):
                    link(v.scalar_tensor_tensor(sc, relu[:, h, :], w_idx[:, r, h:h + 1], sc, ALU.mult, ALU.add))
                own = sc[:, r * P:(r + 1) * P]
                link(v.tensor_tensor(own, own, noncausal, ALU.add))
                for _ in range(TOPK // 8):
                    link(v.max(top8, sc))
                    link(v.match_replace(sc, top8, sc, TAKEN))
                link(v.tensor_scalar(sc, sc, TAKEN, DROPPED, ALU.not_equal, ALU.mult))
                v.tensor_tensor(own, own, noncausal, ALU.add).then_inc(masks_ready, 1)

            take_low(2)
            take_low(3)
            top_keys(1, 1, score1, relu1)
            take_low(4)
            chunk_done(2)
            for a in range(2):
                rows = slice(a * AD, (a + 1) * AD)
                last = v.tensor_copy(kblk[rows, :, a, :], proj(2)[rows, :].rearrange("p (m t) -> p m t", m=4))
            last.then_inc(evacuated[0], 1)
            top_keys(2, 0, score0, relu0)
            take_low(5)

            take_low(6)
            dve.wait_ge(sig_ready, 1)
            v.scalar_tensor_tensor(hq, proj(4), BD ** -0.5, hq, ALU.mult, ALU.mult).then_inc(evacuated[0], 1)
            take_low(7)
            dve.wait_ge(evacuated[1], 3)
            for h in range(BH):
                fh = hf[:, h * S:(h + 1) * S]
                last = v.tensor_scalar(fh, fh, lb_rest[:, h:h + 1], lb[:, h:h + 1], ALU.mult, ALU.add)
            link(last)
            v.tensor_scalar(hk, hf, -1.0, 1.0, ALU.mult, ALU.add).then_inc(hgrn_ready, 1)

            for n, (r, bias) in enumerate(((1, bias1), (0, bias0))):
                keys = (r + 1) * P
                dve.wait_ge(logits_mm, n + 1)
                dve.wait_ge(bias_ready, n + 1)
                v.scalar_tensor_tensor(probs[r], banks(4, 8)[:, 0:AH * keys].rearrange("p (h s) -> p h s", h=AH),
                                       AD ** -0.5, bias, ALU.mult, ALU.add).then_inc(logits_ready, 1)
                dve.wait_ge(logits_ready, n + 1)
                link(v.tensor_reduce(row_max[r], probs[r], AX.X, ALU.max))
                v.tensor_scalar(row_max[r], row_max[r], -1.0, None, ALU.mult).then_inc(max_ready, 1)

            dve.wait_ge(diag_mm, 1)
            dve.wait_ge(consts_in, 16)
            link(v.tensor_tensor(mixT, banks(6, 8).rearrange("p (g t) -> p g t", t=P),
                                 bc(ident.unsqueeze(1), [P, BH * NT, P]), ALU.mult))
            v.tensor_tensor(hq, hq, hf, ALU.mult).then_inc(level_ready, 1)
            take_low(8)
            dve.wait_ge(level_ready, 1)
            offset = [0]
            products = hf

            def next_level(l, products):
                dve.wait_ge(level_mm, l + 1)
                size = 1 << l
                if l == LEVELS:
                    v.tensor_copy(crossT, psum[:, 6 + l % 2, :].rearrange("p (h t) -> p h t", h=BH)).then_inc(mix_ready, 1)
                    return None
                odd = mixT.rearrange("p g (n a l) -> p g n a l", a=2, l=size)[:, :, :, 1, :]
                mask = lvl[:, l * 64:(l + 1) * 64].rearrange("p (n l) -> p n l", l=size)
                data = psum[:, 6 + l % 2, :].rearrange("p (g n l) -> p g n l", g=BH * NT, l=size)
                n = 64 // size
                v.copy_predicated(odd, bc(mask.unsqueeze(1), [P, BH * NT, n, size]), data)
                pairs = products.rearrange("p (n a) -> p n a", a=2)
                nb = 512 // size
                q2 = hq.rearrange("p (n a l) -> p n a l", a=2, l=size)
                k2 = hk.rearrange("p (n a l) -> p n a l", a=2, l=size)
                grown = hprod[:, offset[0]:offset[0] + nb]
                offset[0] += nb
                v.tensor_tensor(q2[:, :, 1, :], q2[:, :, 1, :], bc(pairs[:, :, 0:1], [P, nb, size]), ALU.mult)
                v.tensor_tensor(grown, pairs[:, :, 0], pairs[:, :, 1], ALU.mult)
                v.tensor_tensor(k2[:, :, 0, :], k2[:, :, 0, :], bc(pairs[:, :, 1:2], [P, nb, size]),
                                ALU.mult).then_inc(level_ready, 1)
                dve.wait_ge(level_ready, l + 2)
                return grown

            def normalise(n, r):
                keys = (r + 1) * P
                dve.wait_ge(exp_ready, n)
                link(v.reciprocal(den[r], den[r]))
                v.tensor_tensor(probs[r], probs[r], bc(den[r].unsqueeze(2), [P, AH, keys]),
                                ALU.mult).then_inc(probs_ready, 1)

            products = next_level(0, products)
            normalise(1, 1)
            products = next_level(1, products)
            take_low(9)
            dve.wait_ge(sig_ready, 2)
            v.tensor_tensor(silu_g[:, :], proj(7), silu_g[:, :], ALU.mult).then_inc(evacuated[1], 1)
            normalise(2, 0)
            for l in range(2, LEVELS + 1):
                products = next_level(l, products)
                if l == 5:
                    dve.wait_ge(ya_ready, 1)
                    v.tensor_tensor(y_a_low, banks(4, 6), y_a_high.bitcast(F32), ALU.subtract).then_inc(y_a_low_ready, 1)
                if l % 2 and l > 2:
                    take_low(10 + (l - 3) // 2)

            dve.wait_ge(o_squared, 1)
            v.tensor_reduce(o_ss, hk.rearrange("p (g e) -> p g e", e=BD), AX.X, ALU.add).then_inc(o_squares, 1)
            dve.wait_ge(o_rs_ready, 1)
            o3 = hq.rearrange("p (g e) -> p g e", e=BD)
            v.tensor_tensor(o3, banks(6, 8).rearrange("p (g e) -> p g e", e=BD),
                            bc(o_rs.unsqueeze(2), [P, NT * BH, BD]), ALU.mult).then_inc(o_normed, 1)
            take_low(13)
            dve.wait_ge(yb_mm, 1)
            for h in range(BH):
                cols = slice(h * S, (h + 1) * S)
                last = v.scalar_tensor_tensor(hf[:, cols], banks(6, 8)[:, cols], g_hgrn[:, h:h + 1], silu_g[:, cols],
                                              ALU.mult, ALU.mult)
            last.then_inc(yb_ready, 1)
            dve.wait_ge(y_b_high_ready, 1)
            v.tensor_tensor(y_b_low, hf, y_b_high.bitcast(F32), ALU.subtract).then_inc(y_b_low_ready, 1)

            for n in range(2):
                dve.wait_ge(evacuated[n], len(ORDER) // 2)
            for m in range(NJ):
                cols = slice(m * S, (m + 1) * S)
                dve.wait_ge(merge_mm, m + 1)
                if m:
                    dve.wait_ge(merge_ready, m)
                v.tensor_tensor(merge_a, psum[:, m % 4, 0:S], sig_a[:, cols], ALU.mult)
                link(v.tensor_tensor(merge_b, psum[:, m % 4, S:2 * S], sig_b[:, cols], ALU.mult))
                v.tensor_tensor(mergedT[:, m, :], merge_a, merge_b, ALU.add).then_inc(merge_ready, 1)
            dve.wait_ge(ffn_gain_in, 16)

            def norm_ffn_half(r, half):
                tiles = slice(4 * half, 4 * half + 4)
                stream = banks(4 + 2 * r, 6 + 2 * r).rearrange("p (q j) -> p j q", j=NJ)
                gain = va_region[:, :].rearrange("p (q j) -> p j q", j=NJ)
                v.scalar_tensor_tensor(h2[:, r, tiles], stream[:, tiles], rs[:, r:r + 1], gain[:, tiles],
                                       ALU.mult, ALU.mult).then_inc(h2_ready, 1)

            def route(r):
                dve.wait_ge(router_mm, r + 1)
                link(v.tensor_tensor(r_logits[:, r, :], psum[:, 2 * r, 0:NE], router_b, ALU.add))
                link(v.max(r_top[:, r, :], r_logits[:, r, :]))
                link(v.max_index(itiny[:, r * 8:(r + 1) * 8], r_top[:, r, :], r_logits[:, r, :]))
                v.tensor_scalar(r_neg[:, r:r + 1], r_top[:, r, 0:1], -1.0, None, ALU.mult).then_inc(router_max, 1)
                link(v.tensor_copy(r_idx[:, r, :], itiny[:, r * 8:(r + 1) * 8]))
                link(v.tensor_tensor(choice[:, r], bc(iota[:, 0:NE].unsqueeze(1), [P, TOP_K, NE]),
                                     bc(r_idx[:, r, 0:TOP_K].unsqueeze(2), [P, TOP_K, NE]), ALU.is_equal))
                v.tensor_reduce(sel[:, r, :], choice[:, r].rearrange("p k e -> p e k"), AX.X, ALU.add).then_inc(sel_ready, 1)

            v.memset(sel_pad[:, NT * NE:], 0.0)
            for r in range(NT):
                dve.wait_ge(rs_ready, NT + r + 1)
                norm_ffn_half(r, 0)
                norm_ffn_half(r, 1)
                dve.wait_ge(h2T_mm, r + 1)
                v.tensor_copy(h2T[:, 0:4, r * P:(r + 1) * P],
                              psum[:, 2 * r, :].rearrange("p (j t) -> p j t", j=4)).then_inc(h2T_ready[r], 1)
            for r in range(NT):
                route(r)
            dve.wait_ge(sel_ready, NT)
            link(v.tensor_scalar(pos, sel, -1.0e4, 1.0e4, ALU.mult, ALU.add))
            dve.wait_ge(pos_mm, 1)
            link(v.tensor_tensor(pos, pos, psum[:, 1, 0:NT * NE].rearrange("p (r e) -> p r e", r=NT), ALU.add))
            for r in range(NT):
                last = v.tensor_scalar(pick[:, r, :], iota[:, 0:SLOTS], pos[:, r, 0:1], None, ALU.is_equal)
            last.then_inc(pick_ready, 1)
            counts = psum[:, 1, 2 * NE:3 * NE]
            link(v.tensor_scalar(n_over, counts, float(SLOTS), None, ALU.is_gt))
            for c in range(2, S // SLOTS):
                link(v.scalar_tensor_tensor(n_over, counts, float(c * SLOTS), n_over, ALU.is_gt, ALU.add))
            link(v.tensor_tensor_scan(cum, n_over, sel_pad[:, NT * NE:], 0.0, ALU.add, ALU.add))
            v.tensor_scalar(table[0:1, 2 * TAB:2 * TAB + 1], cum[0:1, NE - 1:NE], float(NE), None,
                            ALU.add).then_inc(n_items_ready, 1)
            link(v.tensor_scalar(le, cum, over_idx, None, ALU.is_le))
            link(v.tensor_reduce(items[:, 0:1], le, AX.X, ALU.add))
            link(v.tensor_tensor(le, le, cum, ALU.mult))
            link(v.tensor_reduce(items[:, 2:3], le, AX.X, ALU.max))
            link(v.tensor_tensor(items[:, 0:1], items[:, 0:1], first_expert, ALU.add))
            link(v.tensor_scalar(items[:, 0:1], items[:, 0:1], float(NE - 1), None, ALU.min))
            link(v.tensor_tensor(items[:, 1:2], over_idx, items[:, 2:3], ALU.subtract))
            link(v.tensor_scalar(items[:, 1:2], items[:, 1:2], 1.0, is_over, ALU.add, ALU.mult))
            v.tensor_scalar(items[:, 1:2], items[:, 1:2], 0.0, float(S // SLOTS - 1), ALU.max,
                            ALU.min).then_inc(items_ready, 1)
            dve.wait_ge(items_mm, 1)
            v.tensor_copy(table[0:1, 0:TAB], psum[0:1, 2, 0:TAB])
            v.tensor_scalar(table[0:1, TAB:2 * TAB], psum[0:1, 2, P:P + TAB], float(SLOTS), None,
                            ALU.mult).then_inc(table_ready, 1)
            dve.wait_ge(table_ready, 1)
            dve.wait_ge(router_exp, 1)
            link(v.reciprocal(r_den, r_den))
            link(v.tensor_tensor(r_gate, r_gate, bc(r_den.unsqueeze(2), [P, NT, TOP_K]), ALU.mult))
            for r in range(NT):
                last = v.tensor_tensor(choice_g[:, r], choice[:, r], bc(r_gate[:, r, :].unsqueeze(2), [P, TOP_K, NE]),
                                       ALU.mult)
            link(last)
            for r in range(NT):
                last = v.tensor_reduce(gates[:, r, :], choice_g[:, r].rearrange("p k e -> p e k"), AX.X, ALU.add)
            link(last)
            dve.wait_ge(padded_zero, 1)

            n_items = dve.value_load(table[0:1, 2 * TAB:2 * TAB + 1], min_val=NE, max_val=MAX_ITEMS)
            with dve.Fori(0, n_items) as i:
                e_next = dve.value_load(table[0:1, bass.ds(i + 1, 1)], min_val=0, max_val=NE - 1)
                s0_next = dve.value_load(table[0:1, bass.ds(i + (TAB + 1), 1)], min_val=0, max_val=S - SLOTS)
                dve.wait_ge(gather_mm, i + 1)
                for r in range(NT):
                    last = v.tensor_scalar(pick[:, r, :], iota[:, bass.ds(s0_next, SLOTS)],
                                           pos[:, r, bass.ds(e_next, 1)], None, ALU.is_equal)
                last.then_inc(pick_ready, 1)
                e = dve.value_load(table[0:1, bass.ds(i, 1)], min_val=0, max_val=NE - 1)
                s0 = dve.value_load(table[0:1, bass.ds(i + TAB, 1)], min_val=0, max_val=S - SLOTS)
                dve.wait_ge(y_mm, i + 1)
                for r in range(NT):
                    v.tensor_scalar(padded[:, r, SLOTS:2 * SLOTS], iota[:, bass.ds(s0, SLOTS)],
                                    pos[:, r, bass.ds(e, 1)], gates[:, r, bass.ds(e, 1)], ALU.is_equal, ALU.mult)
                v.tensor_copy(which_expert, bc(ident[:, bass.ds(e, 1)], [P, SLOTS])).then_inc(padded_ready, 1)
                dve.wait_ge(w_used[MOE_SLOT[3]], i + (USED_BEFORE[MOE_SLOT[3]] + 1))
                v.tensor_scalar(gate_sb, psum[:, 0, :], LIMIT, None, ALU.min).then_inc(gate_ready, 1)
                v.tensor_scalar(lin_sb, psum[:, 1, :], LIMIT, -LIMIT, ALU.min, ALU.max).then_inc(moe_dve, 1)
                dve.wait_ge(moe_dve, i * 2 + 1)
                v.scalar_tensor_tensor(lin_sb, lin_sb, 1.0, gate_sb, ALU.add, ALU.mult).then_inc(moe_dve, 1)
                dve.wait_ge(moe_dve, i * 2 + 2)
                dve.wait_ge(sigm_ready, i + 1)
                v.tensor_tensor(act_sb, lin_sb, sig_sb, ALU.mult).then_inc(act_ready, 1)

            dve.wait_ge(final_gain_in, 16)
            for r in range(NT):
                dve.wait_ge(final_rs, r + 1)
                for half in range(2):
                    cols = slice(half * 512, (half + 1) * 512)
                    v.scalar_tensor_tensor(xr[:, r, cols], psum[:, 4 + 2 * r + half, :], rs[:, r:r + 1],
                                           vb_region[:, cols], ALU.mult, ALU.mult).then_inc(out_ready, 1)

        @block.gpsimd
        def _(pool):
            g = nc.gpsimd
            steps = [0]

            def root(dst, src, width, n, done):
                g.tensor_scalar(src, src, 1.0 / width, EPS, ALU.mult, ALU.add).then_inc(pool_step, 1)
                steps[0] += 1
                pool.wait_ge(pool_step, steps[0])
                g.tensor_tensor(dst, src, minus_half.broadcast_to([P, n]), ALU.pow).then_inc(done, 1)

            g.memset(row_max[0][:, 0:1], 0.0)
            g.memset(idx_region[:, 512:1024], 0.0).then_inc(cell_zero, 1)
            g.memset(idx_region[:, 1024:1536], 0.0).then_inc(blocks_zero, 1)
            g.memset(qk_region[:, 1024:3072], 0.0).then_inc(blocks_zero, 1)
            pool.wait_ge(consts_in, 16)
            for r in range(NT):
                pool.wait_ge(squares, r + 1)
                root(rs[:, r:r + 1], ss[:, r:r + 1], D, 1, rs_ready)

            def take_low(n):
                pool.wait_ge(high_ready, n)
                cols = slice(0, POOL_COLS)
                g.tensor_tensor(slot_r[slot_of(n)][:, cols], ring[:, slot_of(n), cols],
                                slot_r[high_slot(n)][:, cols].bitcast(F32), ALU.subtract).then_inc(low_pool, 1)

            for n in range(1, 5):
                take_low(n)
            pool.wait_ge(bias_in, 32)
            for n, (sc, bias, keys) in enumerate(((score1, bias1, S), (score0, bias0, P))):
                pool.wait_ge(masks_ready, n + 1)
                g.tensor_tensor(bias, bias, sc.unsqueeze(1).broadcast_to([P, AH, keys]), ALU.add).then_inc(bias_ready, 1)
                take_low(5 + n)
            for n in range(7, 11):
                take_low(n)
            pool.wait_ge(ya_mm, 1)
            g.memset(bias_region[:, :], 0.0).then_inc(moe_bias_zero, 1)
            take_low(11)
            take_low(12)
            pool.wait_ge(o_squares, 1)
            root(o_rs, o_ss, BD, NT * BH, o_rs_ready)
            take_low(13)
            pool.wait_ge(x_high_ready, 2)
            g.tensor_tensor(x_low, x_sb[:, :], x_high.bitcast(F32), ALU.subtract).then_inc(x_low_ready, 1)
            pool.wait_ge(merge_mm, NJ)
            g.memset(padded, 0.0).then_inc(padded_zero, 1)
            g.memset(y_sb, 0.0).then_inc(y_ready, 1)
            g.memset(combT_sb, 0.0).then_inc(combT_ready, 1)

            def mean_root(r, done):
                g.tensor_scalar(ms[:, 2 * r:2 * r + 1], ms[:, 2 * r:2 * r + 1], ms[:, 2 * r + 1:2 * r + 2], EPS,
                                ALU.add, ALU.add).then_inc(pool_step, 1)
                steps[0] += 1
                pool.wait_ge(pool_step, steps[0])
                g.tensor_tensor(rs[:, r:r + 1], ms[:, 2 * r:2 * r + 1], minus_half, ALU.pow).then_inc(done, 1)

            for r in range(NT):
                pool.wait_ge(squares, NT + 2 * (r + 1))
                mean_root(r, rs_ready)
            for r in range(NT):
                pool.wait_ge(final_ss, 2 * (r + 1))
                mean_root(r, final_rs)


INPUTS = ["x", "w_in", "w_up_a", "w_up_b", "w_out", "norm_mix", "norm_ffn", "norm_final", "hgrn_norm",
          "lb_logits", "rel_bias", "w_router", "b_router", "w_gu", "b_gu", "w_down", "b_down"]


def kernel(**inputs):
    import concourse.bacc as bacc
    from concourse.bass_utils import run_bass_kernel_spmd as run

    nc = bacc.Bacc("TRN2", target_bir_lowering=False, num_devices=1)
    arrays = {f"in_{n}": np.ascontiguousarray(inputs[n]) for n in INPUTS}
    arrays["in_lb_logits"] = np.ascontiguousarray(
        inputs["lb_logits"].reshape(2, BH, P).transpose(2, 0, 1).reshape(P, 2 * BH))
    arrays["in_hgrn_norm"] = np.ascontiguousarray(inputs["hgrn_norm"][0].T)
    for name, a in zip(("consts", "levels", "onehot"), shape_constants()):
        arrays[f"in_{name}"] = a
    args = [nc.dram_tensor(n, a.shape, mybir.dt.from_np(a.dtype), kind="ExternalInput").ap()
            for n, a in arrays.items()]
    out = nc.dram_tensor("out_y", inputs["x"].shape, F32, kind="ExternalOutput").ap()
    build(nc, *args, out)
    return run(nc, [arrays], core_ids=[0]).results[0]["out_y"]
```
